# Optimizing a Trainium2 kernel written in Bass

```python
import math
import jax
import jax.numpy as jnp
from jax import lax
import numpy as np

D_MODEL = 1024
BATCH = 1
SEQ = 512
DEPTH = 2
DEC_BATCH = 8
DEC_SEQ = 1
PAST_LEN = 4096
PAGE_SIZE = 128

N_EVEN = (DEPTH + 1) // 2
N_ODD = DEPTH // 2
DA_HEADS = 4
DA_DH = 64
DA_VD = 2 * DA_DH
GLA_HEADS = 4
GLA_DK = 64
GLA_DV = 128
GLA_RANK = 16
GLA_TAU = 16.0
GLA_CHUNK = 16
DA_QK = DA_HEADS * 2 * DA_DH
DA_V = DA_HEADS * DA_VD
GLA_QK = GLA_HEADS * GLA_DK
GLA_V = GLA_HEADS * GLA_DV
SPLIT_SIZES = (DA_QK, DA_QK, DA_V, GLA_QK, GLA_QK, GLA_V, GLA_RANK, GLA_V)
D_IN_EVEN = sum(SPLIT_SIZES)
D_MIX = DA_V + GLA_V
D_RNN = D_MODEL
RNN_BLOCKS = 8
RNN_BW = D_RNN // RNN_BLOCKS
CONV_W = 4
RG_C = 8.0
D_FF = 4 * D_MODEL
NUM_BUCKETS = 32
MAX_DISTANCE = 128
Q_BLOCK = 128
EPS = 1e-6
NEG = -1e30

kernel_name = 'hybrid_diffattn_gla_rglru_decode_step'

def rmsnorm(x, g):
    xf = x.astype(jnp.float32)
    y = xf * lax.rsqrt(jnp.mean(xf * xf, axis=-1, keepdims=True) + EPS)
    return (y * g.astype(jnp.float32)).astype(x.dtype)

def t5_bucket(rel):
    rel = jnp.maximum(rel, 0)
    max_exact = NUM_BUCKETS // 2
    large = max_exact + (jnp.log(jnp.maximum(rel, 1).astype(jnp.float32) / max_exact)
                         / math.log(MAX_DISTANCE / max_exact) * (NUM_BUCKETS - max_exact)).astype(jnp.int32)
    large = jnp.minimum(large, NUM_BUCKETS - 1)
    return jnp.where(rel < max_exact, rel, large)

def rel_bias(table, qpos, kpos):
    bucket = t5_bucket(qpos[:, None] - kpos[None, :])
    return jnp.transpose(table[bucket], (2, 0, 1)).astype(jnp.float32)

def diff_lambda(lq1, lk1, lq2, lk2, lam_init):
    f = jnp.float32
    return (jnp.exp(jnp.sum(lq1.astype(f) * lk1.astype(f)))
            - jnp.exp(jnp.sum(lq2.astype(f) * lk2.astype(f))) + lam_init)

def diff_probs(l1, l2, lam):
    return jax.nn.softmax(l1, axis=-1) - lam * jax.nn.softmax(l2, axis=-1)

def diff_attn_prompt(q, k, v, lam, table):
    B, T = q.shape[:2]
    q1, q2 = jnp.split(q, 2, axis=-1)
    k1, k2 = jnp.split(k, 2, axis=-1)
    kpos = jnp.arange(T)
    scale = DA_DH ** -0.5

    def block(i):
        start = i * Q_BLOCK
        qb1 = lax.dynamic_slice_in_dim(q1, start, Q_BLOCK, axis=1)
        qb2 = lax.dynamic_slice_in_dim(q2, start, Q_BLOCK, axis=1)
        qpos = start + jnp.arange(Q_BLOCK)
        bias = rel_bias(table, qpos, kpos)
        mask = qpos[:, None] >= kpos[None, :]
        l1 = jnp.where(mask, jnp.einsum('bqhd,bkhd->bhqk', qb1, k1).astype(jnp.float32) * scale + bias, NEG)
        l2 = jnp.where(mask, jnp.einsum('bqhd,bkhd->bhqk', qb2, k2).astype(jnp.float32) * scale + bias, NEG)
        a = diff_probs(l1, l2, lam)
        return jnp.einsum('bhqk,bkhd->bqhd', a, v.astype(jnp.float32))

    out = lax.map(block, jnp.arange(T // Q_BLOCK))
    return jnp.moveaxis(out, 0, 1).reshape(B, T, DA_HEADS, DA_VD).astype(q.dtype)

def diff_attn_sample(q, k_new, v_new, k_past, v_past, lam, table):
    T = q.shape[1]
    P = k_past.shape[1]
    q1, q2 = jnp.split(q, 2, axis=-1)
    kn1, kn2 = jnp.split(k_new, 2, axis=-1)
    kp1, kp2 = jnp.split(k_past, 2, axis=-1)
    scale = DA_DH ** -0.5
    qpos = P + jnp.arange(T)
    bias_p = rel_bias(table, qpos, jnp.arange(P))
    bias_n = rel_bias(table, qpos, qpos)
    mask_n = qpos[:, None] >= qpos[None, :]

    def logits(qh, kp, kn):
        lp = jnp.einsum('bqhd,bkhd->bhqk', qh, kp).astype(jnp.float32) * scale + bias_p
        ln = jnp.where(mask_n, jnp.einsum('bqhd,bkhd->bhqk', qh, kn).astype(jnp.float32) * scale + bias_n, NEG)
        return jnp.concatenate([lp, ln], axis=-1)

    a = diff_probs(logits(q1, kp1, kn1), logits(q2, kp2, kn2), lam)
    out = (jnp.einsum('bhqk,bkhd->bqhd', a[..., :P], v_past.astype(jnp.float32))
           + jnp.einsum('bhqk,bkhd->bqhd', a[..., P:], v_new.astype(jnp.float32)))
    return out.astype(q.dtype)

def gla_recurrence(q, k, v, log_a, s0):
    B, T, H, DK = q.shape
    DV = v.shape[-1]
    C = GLA_CHUNK if T % GLA_CHUNK == 0 else 1
    nc = T // C
    f = jnp.float32

    def chunks(t):
        return jnp.moveaxis(t.reshape(B, nc, C, *t.shape[2:]), 1, 0)

    bcum = jnp.cumsum(chunks(log_a), axis=2)
    causal = jnp.tril(jnp.ones((C, C), dtype=bool))

    def step(S, inp):
        qc, kc, vc, bc = inp
        qe = qc.astype(f) * jnp.exp(bc)
        ke = kc.astype(f) * jnp.exp(-bc)
        att = jnp.where(causal, jnp.einsum('bchk,bshk->bhcs', qe, ke), 0.0)
        o = jnp.einsum('bhcs,bshv->bchv', att, vc.astype(f)) + jnp.einsum('bchk,bhkv->bchv', qe, S)
        b_last = bc[:, -1]
        kd = kc.astype(f) * jnp.exp(b_last[:, None] - bc)
        S = jnp.exp(b_last)[..., None] * S + jnp.einsum('bshk,bshv->bhkv', kd, vc.astype(f))
        return S, o

    S, o = lax.scan(step, s0.astype(f), (chunks(q), chunks(k), chunks(v), bcum))
    return jnp.moveaxis(o, 0, 1).reshape(B, T, H, DV), S

def even_mixer(h, w_in, w_a2, b_a2, g_da, g_gla, w_out, lam_init, gla_s0, attend):
    B, T, _ = h.shape
    offs = [int(o) for o in np.cumsum(SPLIT_SIZES)[:-1]]
    da_q, da_k, da_v, g_q, g_k, g_v, g_lr, g_og = jnp.split(h @ w_in, offs, axis=-1)
    da_q = da_q.reshape(B, T, DA_HEADS, 2 * DA_DH)
    da_k = da_k.reshape(B, T, DA_HEADS, 2 * DA_DH)
    da_v = da_v.reshape(B, T, DA_HEADS, DA_VD)
    a_out = rmsnorm(attend(da_q, da_k, da_v), g_da) * (1.0 - lam_init)
    log_a = jax.nn.log_sigmoid((g_lr @ w_a2 + b_a2).astype(jnp.float32)) / GLA_TAU
    gq = g_q.reshape(B, T, GLA_HEADS, GLA_DK) * (GLA_DK ** -0.5)
    o, s_new = gla_recurrence(gq, g_k.reshape(B, T, GLA_HEADS, GLA_DK), g_v.reshape(B, T, GLA_HEADS, GLA_DV),
                              log_a.reshape(B, T, GLA_HEADS, GLA_DK), gla_s0)
    o = rmsnorm(o.astype(h.dtype), g_gla) * jax.nn.silu(g_og).reshape(B, T, GLA_HEADS, GLA_DV)
    mix = jnp.concatenate([a_out.reshape(B, T, DA_V), o.reshape(B, T, GLA_V)], axis=-1)
    return (mix @ w_out).astype(h.dtype), da_k, da_v, s_new.astype(h.dtype)

def linear_scan(a, b, h0):
    b = b.at[:, 0].add(a[:, 0] * h0.astype(jnp.float32))

    def combine(l, r):
        al, bl = l
        ar, br = r
        return al * ar, ar * bl + br

    _, hs = lax.associative_scan(combine, (a, b), axis=1)
    return hs

def odd_mixer(h, w_in, conv_w, conv_b, w_ga, b_ga, w_gx, b_gx, lam_rg, w_out, conv_buf, h0):
    B, T, _ = h.shape
    gate_br, x_br = jnp.split(h @ w_in, 2, axis=-1)
    xp = jnp.concatenate([conv_buf.astype(x_br.dtype), x_br], axis=1)
    xc = conv_b + sum(conv_w[j] * xp[:, j:j + T] for j in range(CONV_W))
    new_buf = xp[:, T:]
    xb = xc.reshape(B, T, RNN_BLOCKS, RNN_BW)
    r = jax.nn.sigmoid((jnp.einsum('btnd,nde->btne', xb, w_ga).reshape(B, T, D_RNN) + b_ga).astype(jnp.float32))
    i = jax.nn.sigmoid((jnp.einsum('btnd,nde->btne', xb, w_gx).reshape(B, T, D_RNN) + b_gx).astype(jnp.float32))
    log_a = -RG_C * jax.nn.softplus(-lam_rg.astype(jnp.float32)) * r
    a = jnp.exp(log_a)
    b = jnp.sqrt(-jnp.expm1(2.0 * log_a)) * (i * xc.astype(jnp.float32))
    hs = linear_scan(a, b, h0)
    y = jax.nn.gelu(gate_br) * hs.astype(h.dtype)
    return (y @ w_out).astype(h.dtype), new_buf, hs[:, -1].astype(h.dtype)

def sq_relu_mlp(h, w_up, w_down):
    return jnp.square(jax.nn.relu(h @ w_up)) @ w_down

def setup_inputs(seed: int = 0) -> dict:
    key = jax.random.key(seed)
    ks = list(jax.random.split(key, 40))
    f32 = jnp.float32

    def nrm(shape, scale):
        return jax.random.normal(ks.pop(), shape, f32) * scale

    n_pages = PAST_LEN // PAGE_SIZE
    n_used = DEC_BATCH * n_pages
    n_pool = n_used + n_used // 4
    page_table = jax.random.permutation(ks.pop(), n_pool)[:n_used].reshape(DEC_BATCH, n_pages).astype(jnp.int32)
    a0 = jax.random.uniform(ks.pop(), (N_ODD, D_RNN), f32, 0.9, 0.999)
    s = a0 ** (1.0 / RG_C)
    rg_lambda = jnp.log(s) - jnp.log1p(-s)
    return {
        'x_prompt': nrm((BATCH, SEQ, D_MODEL), 1.0),
        'x_sample': nrm((DEC_BATCH, DEC_SEQ, D_MODEL), 1.0),
        'cache_k': nrm((N_EVEN, n_pool, PAGE_SIZE, DA_HEADS, 2 * DA_DH), 1.0),
        'cache_v': nrm((N_EVEN, n_pool, PAGE_SIZE, DA_HEADS, DA_VD), 1.0),
        'state_gla': nrm((N_EVEN, DEC_BATCH, GLA_HEADS, GLA_DK, GLA_DV), 0.5),
        'state_conv': nrm((N_ODD, DEC_BATCH, CONV_W - 1, D_RNN), 1.0),
        'state_rglru': nrm((N_ODD, DEC_BATCH, D_RNN), 1.0),
        'page_table': page_table,
        'rel_table': nrm((NUM_BUCKETS, DA_HEADS), 0.5),
        'norm_g': 1.0 + nrm((DEPTH, 4, D_MODEL), 0.05),
        'w_up': nrm((DEPTH, D_MODEL, D_FF), D_MODEL ** -0.5),
        'w_down': nrm((DEPTH, D_FF, D_MODEL), D_FF ** -0.5),
        'w_in_even': nrm((N_EVEN, D_MODEL, D_IN_EVEN), D_MODEL ** -0.5),
        'w_alpha2': nrm((N_EVEN, GLA_RANK, GLA_QK), GLA_RANK ** -0.5),
        'b_alpha2': nrm((N_EVEN, GLA_QK), 0.5),
        'lam_q1': nrm((N_EVEN, DA_DH), 0.1),
        'lam_k1': nrm((N_EVEN, DA_DH), 0.1),
        'lam_q2': nrm((N_EVEN, DA_DH), 0.1),
        'lam_k2': nrm((N_EVEN, DA_DH), 0.1),
        'g_diff': 1.0 + nrm((N_EVEN, DA_VD), 0.05),
        'g_gla': 1.0 + nrm((N_EVEN, GLA_DV), 0.05),
        'w_out_even': nrm((N_EVEN, D_MIX, D_MODEL), D_MIX ** -0.5),
        'w_in_odd': nrm((N_ODD, D_MODEL, 2 * D_RNN), D_MODEL ** -0.5),
        'conv_w': nrm((N_ODD, CONV_W, D_RNN), CONV_W ** -0.5),
        'conv_b': nrm((N_ODD, D_RNN), 0.02),
        'w_gate_a': nrm((N_ODD, RNN_BLOCKS, RNN_BW, RNN_BW), RNN_BW ** -0.5),
        'b_gate_a': nrm((N_ODD, D_RNN), 0.02),
        'w_gate_x': nrm((N_ODD, RNN_BLOCKS, RNN_BW, RNN_BW), RNN_BW ** -0.5),
        'b_gate_x': nrm((N_ODD, D_RNN), 0.02),
        'rg_lambda': rg_lambda,
        'w_out_odd': nrm((N_ODD, D_RNN, D_MODEL), D_RNN ** -0.5),
    }

def reference(x_prompt, x_sample, cache_k, cache_v, state_gla, state_conv, state_rglru, page_table,
              rel_table, norm_g, w_up, w_down, w_in_even, w_alpha2, b_alpha2, lam_q1, lam_k1, lam_q2, lam_k2,
              g_diff, g_gla, w_out_even, w_in_odd, conv_w, conv_b, w_gate_a, b_gate_a, w_gate_x, b_gate_x,
              rg_lambda, w_out_odd):
    Bp = x_prompt.shape[0]
    Bd = x_sample.shape[0]
    P = page_table.shape[1] * PAGE_SIZE
    yp, ys = x_prompt, x_sample
    kp_l, vp_l, ks_l, vs_l, gp_l, gs_l = [], [], [], [], [], []
    cp_l, cs_l, rp_l, rs_l = [], [], [], []
    for layer in range(DEPTH):
        g = norm_g[layer]
        hp = rmsnorm(yp, g[0])
        hs = rmsnorm(ys, g[0])
        if layer % 2 == 0:
            li = layer // 2
            lam_init = 0.8 - 0.6 * math.exp(-0.3 * layer)
            lam = diff_lambda(lam_q1[li], lam_k1[li], lam_q2[li], lam_k2[li], lam_init)
            prm = (w_in_even[li], w_alpha2[li], b_alpha2[li], g_diff[li], g_gla[li], w_out_even[li], lam_init)
            s0_p = jnp.zeros((Bp, GLA_HEADS, GLA_DK, GLA_DV), jnp.float32)
            mp, kpn, vpn, sp = even_mixer(hp, *prm, s0_p,
                                          lambda q, k, v: diff_attn_prompt(q, k, v, lam, rel_table))
            k_past = cache_k[li, page_table].reshape(Bd, P, DA_HEADS, 2 * DA_DH)
            v_past = cache_v[li, page_table].reshape(Bd, P, DA_HEADS, DA_VD)
            ms, ksn, vsn, ss = even_mixer(hs, *prm, state_gla[li],
                                          lambda q, k, v: diff_attn_sample(q, k, v, k_past, v_past, lam, rel_table))
            kp_l.append(kpn); vp_l.append(vpn); ks_l.append(ksn); vs_l.append(vsn)
            gp_l.append(sp); gs_l.append(ss)
        else:
            li = layer // 2
            prm = (w_in_odd[li], conv_w[li], conv_b[li], w_gate_a[li], b_gate_a[li], w_gate_x[li], b_gate_x[li],
                   rg_lambda[li], w_out_odd[li])
            mp, cpn, rpn = odd_mixer(hp, *prm, jnp.zeros((Bp, CONV_W - 1, D_RNN), hp.dtype),
                                     jnp.zeros((Bp, D_RNN), jnp.float32))
            ms, csn, rsn = odd_mixer(hs, *prm, state_conv[li], state_rglru[li])
            cp_l.append(cpn); cs_l.append(csn); rp_l.append(rpn); rs_l.append(rsn)
        yp = yp + rmsnorm(mp, g[1])
        ys = ys + rmsnorm(ms, g[1])
        yp = yp + rmsnorm(sq_relu_mlp(rmsnorm(yp, g[2]), w_up[layer], w_down[layer]), g[3])
        ys = ys + rmsnorm(sq_relu_mlp(rmsnorm(ys, g[2]), w_up[layer], w_down[layer]), g[3])
    k_prompt = jnp.stack(kp_l)
    v_prompt = jnp.stack(vp_l)
    k_sample = jnp.stack(ks_l)
    v_sample = jnp.stack(vs_l)
    gla_prompt = jnp.stack(gp_l)
    gla_sample = jnp.stack(gs_l)
    conv_prompt = jnp.stack(cp_l)
    conv_sample = jnp.stack(cs_l)
    rglru_prompt = jnp.stack(rp_l)
    rglru_sample = jnp.stack(rs_l)
    return (yp, ys, k_prompt, v_prompt, k_sample, v_sample, gla_prompt, gla_sample,
            conv_prompt, conv_sample, rglru_prompt, rglru_sample)


_drawn_inputs = setup_inputs


def setup_inputs(seed=0):
    import zlib

    import numpy as np

    out = dict(_drawn_inputs(seed))
    spreads = {}
    factors = {'lam_q1': 200.0,
     'b_gate_a': 8.0,
     'b_gate_x': 7.491,
     'lam_k1': 4.788,
     'lam_q2': 8.0,
     'lam_k2': 8.0}
    for name, (base, spread) in spreads.items():
        noise = np.random.default_rng([zlib.crc32(name.encode()), seed]).standard_normal(out[name].shape)
        drawn = base * np.exp(spread * noise) if base else spread * noise
        out[name] = jnp.asarray(drawn.astype(out[name].dtype))
    for name, factor in factors.items():
        out[name] = (out[name] * factor).astype(out[name].dtype)
    return out
```

```python
import math
from contextlib import ExitStack

import numpy as np
import concourse.bass as bass
from concourse import mybir

F32 = mybir.dt.float32
F32R = mybir.dt.float32r
I32 = mybir.dt.int32
ALU = mybir.AluOpType
ACT = mybir.ActivationFunctionType
AX = mybir.AxisListType

P = 128
D_MODEL = 1024
SEQ = 512
N_SAMPLE = 8
T = SEQ + N_SAMPLE
HALF = T // 2
KT = D_MODEL // P
N_POOL, PAGE, N_PAGES = 320, 128, 32
HEADS, DH = 4, 64
SCALE = DH ** -0.5
GLA_CHUNK, GLA_TAU, RANK = 16, 16.0, 16
D_IN = 3088
D_FF = 4096
BUCKETS, MAX_DISTANCE = 32, 128
EPS = 1e-6
NEG = -1e30
LAM_INIT = 0.8 - 0.6 * math.exp(0.0)
RG_C = 8.0
CONV_W = 4
SQUARE_OVERFLOWS = 2.0 ** 64

GREV = 640
C_IDENT, C_ATT, C_CHUNK, C_GROUP, C_SEL, C_HOT = 0, 128, 256, 264, 268, 268 + 256
C_EXCH = C_HOT + GREV
C_COLS = C_EXCH + P


def constant_table():
    c = np.zeros((P, C_COLS), np.float32)
    p = np.arange(P)
    c[:, C_IDENT:C_IDENT + P] = np.eye(P)
    s, t = p[:, None], p[None, :]
    c[:, C_ATT:C_ATT + P] = (s <= t) & (s // GLA_CHUNK == t // GLA_CHUNK)
    c[p, C_EXCH + 127 - p] = 1
    c[p, C_CHUNK + p // GLA_CHUNK] = 1
    c[p, C_GROUP + p // N_PAGES] = 1
    for g in range(2):
        c[4 * g + p // N_PAGES, C_SEL + P * g + p] = 1
    rel = 511 - np.arange(GREV)
    exact = BUCKETS // 2
    far = exact + (np.log(np.maximum(rel, 1).astype(np.float32) / exact)
                   / math.log(MAX_DISTANCE / exact) * (BUCKETS - exact)).astype(np.int32)
    bucket = np.where(rel < exact, rel, np.minimum(far, BUCKETS - 1))
    bucket = np.where(rel < 0, BUCKETS, bucket)
    c[bucket, C_HOT + np.arange(GREV)] = 1
    return c


IN_CHUNKS = 13
C_OUT0 = IN_CHUNKS
C_MLP0 = C_OUT0 + 4
C_IN1 = C_MLP0 + 32
C_OUT1 = C_IN1 + 8
C_MLP1 = C_OUT1 + 4
N_CHUNKS = C_MLP1 + 32


def first_tile(c):
    return 2 * c if c < IN_CHUNKS else 2 * c - 1


class Chunk:

    def __init__(self, c, g=None):
        self.static = c
        self.slot = c % 2
        self.count = 1 if c == IN_CHUNKS - 1 else 2
        at = lambda value, per_group: value if g is None else g * per_group + value
        self.ready = at(c + 1, 8)
        self.loaded = at(16 * (c // 2 + 1), 64)
        self.slot_free = at(c - 1, 8)
        self.prev_done = at(first_tile(c - 1) if c >= 2 else 0, 16)
        self.tiles = [first_tile(c) + i for i in range(self.count)]
        self.par = [m % 2 for m in self.tiles]
        self.done = [at(m + 1, 16) for m in self.tiles]
        self.banks_free = [at(m // 2, 8) for m in self.tiles]


def trunk(nc, ctx, a, o):
    x_in = a["x_prompt"][0]
    xs_in = a["x_sample"].rearrange("b t d -> (b t) d")
    cache = {"k": a["cache_k"], "v": a["cache_v"]}
    cache = {n: c.rearrange("l n (c q) h d -> (l n c) (q h d)", q=4) for n, c in cache.items()}

    base = -(-nc.sbuf_base // 64) * 64
    top = [base]

    def region(size):
        at = top[0]
        top[0] += -(-size // 32) * 32
        assert top[0] <= nc.sbuf_usable_end, top[0]
        return at

    def sb(name, shape, dt, at):
        return nc.alloc_sbuf_tensor_at(name, shape, dt, offset=at)

    TB = 4 * T
    X = sb("X", [P, KT, T], F32, region(KT * TB))
    r_h = region(2 * KT * TB)
    r_raw = region(2 * 8192)
    r_w = region(4 * 8192)
    r_1 = region(3 * KT * TB)
    r_kv = region(2 * KT * TB)
    r_t = region(20736)
    r_c = region(0)

    H_hi = sb("H_hi", [P, KT, T], F32R, r_h)
    H_lo = sb("H_lo", [P, KT, T], F32R, r_h + KT * TB)
    RAW = sb("RAW", [P, 2, KT, 256], F32, r_raw)
    W_hi = sb("W_hi", [P, 2, KT, 256], F32R, r_w)
    W_lo = sb("W_lo", [P, 2, KT, 256], F32R, r_w + 16384)

    XIN = sb("XIN", [P, 4, D_MODEL], F32, r_1)
    XSIN = sb("XSIN", [N_SAMPLE, D_MODEL], F32, r_1 + 16384)
    VROWS = sb("VROWS", [P, P], F32, r_1 + 20480)
    VROWS2 = sb("VROWS2", [4, P], F32, r_1 + 20992)
    SROWS = sb("SROWS", [32, D_MODEL], F32, r_1 + 21504)
    LAMIN = sb("LAMIN", [P, 4, DH], F32, r_1 + 25600)
    LAMPR = sb("LAMPR", [P, 2, DH], F32, r_1 + 26624)
    HOT = sb("HOT", [33, GREV], F32, r_1 + 27648)
    GSB = sb("GSB", [4, GREV], F32, r_1 + 30720)
    PJ = sb("PJ", [P, 24, T], F32, r_1)
    U_hi = sb("U_hi", [P, KT, T], F32R, r_1)
    U_lo = sb("U_lo", [P, KT, T], F32R, r_1 + KT * TB)
    ACC = sb("ACC", [P, KT, T], F32, r_1 + 2 * KT * TB)
    GX = sb("GX", [P, 2 * KT, T], F32, r_1)
    RG = ACC

    KV = sb("KV", [P, 4, 4, 512], F32, r_kv)
    DEC = sb("DEC", [P, KT, T], F32, r_kv)
    INP = sb("INP", [P, KT, T], F32, r_kv + KT * TB)
    PROD = sb("PROD", [P, 2, 2, 512], F32, r_t)
    SC = [sb(f"SC{g}", [P, 8, PAGE], F32, r_t + 8192 + 4096 * g) for g in range(2)]
    LR = sb("LR", [P, T], F32, r_t + 12288)
    QB = sb("QB", [P, 2, 512], F32, r_t + 16384)
    SQ = sb("SQ", [P, 2, T], F32, r_t)
    TMP = sb("TMP", [P, 2, T], F32, r_t + 2 * TB)
    RS = sb("RS", [P, 2, T], F32, r_t + 4 * TB)
    UF = sb("UF", [P, 2, T], F32, r_t + 6 * TB)
    RL = SQ
    XC = UF
    YT = sb("YT", [P, 2, D_MODEL], F32, r_kv)
    YS = sb("YS", [N_SAMPLE, D_MODEL], F32, r_kv + 8192)
    WG = [sb(f"WG{i}", [P, KT, P], F32, r_w + 4096 * i) for i in range(2)]

    VT = sb("VT", [P, 4, 512], F32, r_w)
    GVT = sb("GVT", [P, 4, 512], F32, r_w + 8192)
    PR = sb("PR", [P, 2, 512], F32, r_w + 16384)
    AD = sb("AD", [P, 512], F32, r_w + 20480)
    AT = sb("AT", [P, 512], F32, r_w + 22528)
    BC = sb("BC", [P, 2, SEQ], F32, r_w + 24576)
    KDM = sb("KDM", [P, 8, P], F32, r_w + 28672)
    KSTAGE = PR
    XL = sb("XL", [P, 3, T], F32, r_w + 16384)
    BIAS = sb("BIAS", [P, HEADS, 512], F32, r_h)
    SBIAS = sb("SBIAS", [P, HEADS, PAGE], F32, r_h + 8192)
    FLIPPED = sb("FLIPPED", [P, HEADS, 512], F32, r_h + 10240)
    EXCHANGE = sb("EXCHANGE", [P, P], F32, r_h + 31744)
    QE = sb("QE", [P, 2, SEQ], F32, r_h + 10240)
    KE = sb("KE", [P, 2, SEQ], F32, r_h + 14336)
    KD = sb("KD", [P, 2, SEQ], F32, r_h + 18432)
    ST = sb("ST", [P, 2, 9, P], F32, r_h + 22528)
    ATTM = sb("ATTM", [P, 2, P], F32, r_h + 31744)

    def small(name, cols, dt=F32, rows=P):
        cols = list(cols) if isinstance(cols, (list, tuple)) else [cols]
        return sb(name, [rows, *cols], dt, region(4 * int(np.prod(cols))))

    CONST = small("CONST", C_HOT)
    IDENT = CONST[:, C_IDENT:C_IDENT + P]
    ATTMASK = CONST[:, C_ATT:C_ATT + P].bitcast(I32)
    CHUNKMASK = CONST[:, C_CHUNK:C_CHUNK + 8]
    GROUPMASK = CONST[:, C_GROUP:C_GROUP + 4]
    ONES = small("ONES", P)
    VEC = small("VEC", P)
    VEC2 = small("VEC2", 4)
    STATE = small("STATE", [KT, 32])
    V_CONVW, V_CONVB, V_BA, V_BX, V_LAM = 64, 96, 104, 112, 120
    EPSC = small("EPSC", 2)
    PIDX = small("PIDX", 2, I32)
    CIDX = [small(f"CIDX{g}", 1, I32) for g in range(2)]
    WA2 = small("WA2", 256, rows=RANK)
    LAM = small("LAM", 4)
    TAB = small("TAB", 4, rows=33)
    TB0 = small("TB0", 4)
    GD8 = small("GD8", 1)
    MX = small("MX", 2)
    NM = small("NM", 2)
    SM = small("SM", 2)
    RR = small("RR", 2)
    ROWMX = small("ROWMX", 8)
    NROW = small("NROW", 8)
    ROWSUM = small("ROWSUM", 8)
    M84 = small("M84", 4, rows=8)
    MEXP = sb("MEXP", [8, 4, 32], F32, r_h + 32768)
    MDIAG = small("MDIAG", [4, 8], rows=8)
    ZS = small("ZS", [4, 8])
    MP = small("MP", [2, 4, 8])
    ZP = small("ZP", [2, 4, 8])
    SN = small("SN", [8, 4, 2])
    MM = small("MM", 64)
    E1 = small("E1", 64)
    E2 = small("E2", 64)
    ZZ = small("ZZ", 64)
    QKP = small("QKP", [HEADS, N_SAMPLE])
    VSC = small("VSC", [HEADS, N_SAMPLE])
    GVC = small("GVC", [HEADS, N_SAMPLE])
    OW = small("OW", [2, HEADS, N_SAMPLE])
    OS = small("OS", [HEADS, N_SAMPLE])
    DECC = small("DECC", [2, 32])
    LAS = small("LAS", [2, 8])
    EAS = small("EAS", [2, 8])
    ENS = small("ENS", [2, 8])
    QES = small("QES", [2, 8])
    KES = small("KES", [2, 8])
    KSS = small("KSS", [2, 8])
    AKS = small("AKS", [2, 8])
    SPC = small("SPC", 8)
    SPT = small("SPT", [2, 8])
    HL = small("HL", [KT, 9])
    S0 = sb("S0", [P, N_SAMPLE, 2, P], F32, r_1 + 8 * TB)
    RSEL = sb("RSEL", [8, 8, P], F32, r_1 + 16 * TB)
    GVTOK = sb("GVTOK", [N_SAMPLE, 512], F32, r_1 + 16 * TB + 4096)
    SCANM = sb("SCANM", [P, SEQ], F32, r_1 + 16 * TB + 6144)
    PM = sb("PM", [P, 2, 16, 4, 8], F32, r_w + 16384)
    KVTOK = sb("KVTOK", [N_SAMPLE, D_MODEL], F32, r_w + 20480)
    QTOK = sb("QTOK", [N_SAMPLE, 512], F32, r_t)
    STOK = sb("STOK", [11, D_MODEL], F32, r_t + 8 * TB)
    WG = [sb(f"WG{i}", [P, KT, P], F32, r_kv + 4096 * i) for i in range(2)]
    HTOK = STOK

    PS = nc.alloc_psum_tensor("PS", [P, 8, 512], F32)

    def sem(name):
        return ctx.enter_context(nc.semaphore(name))

    act_step = sem("act_step")
    ad_ready = sem("ad_ready")
    at_copied = sem("at_copied")
    at_done = sem("at_done")
    att_done = sem("att_done")
    attm_ready = sem("attm_ready")
    bc_ready = sem("bc_ready")
    bias_loaded = sem("bias_loaded")
    bias_ready = sem("bias_ready")
    cidx_ready = sem("cidx_ready")
    const_loaded = sem("const_loaded")
    dve_step = sem("dve_step")
    eb_ready = sem("eb_ready")
    em_ready = sem("em_ready")
    ex_done = sem("ex_done")
    flip_done = sem("flip_done")
    g_done = sem("g_done")
    gates_done = sem("gates_done")
    gates_loaded = sem("gates_loaded")
    gelu_ready = sem("gelu_ready")
    go_copied = sem("go_copied")
    go_done = sem("go_done")
    go_s_ready = sem("go_s_ready")
    gs_done = sem("gs_done")
    gs_v_done = sem("gs_v_done")
    gs_v_used = sem("gs_v_used")
    h_ready = sem("h_ready")
    hf_ready = sem("hf_ready")
    hhi_ready = sem("hhi_ready")
    hl_ready = sem("hl_ready")
    hrows_copied = sem("hrows_copied")
    hrows_done = sem("hrows_done")
    i_ready = sem("i_ready")
    idx_loaded = sem("idx_loaded")
    inverse_ready = sem("inverse_ready")
    ix_ready = sem("ix_ready")
    k_used = sem("k_used")
    kd_ready = sem("kd_ready")
    kdm_ready = sem("kdm_ready")
    kdt_done = sem("kdt_done")
    kdx_exp = sem("kdx_exp")
    kdx_ready = sem("kdx_ready")
    la_done = sem("la_done")
    lam_exp = sem("lam_exp")
    lam_loaded = sem("lam_loaded")
    lam_sums = sem("lam_sums")
    ln_ready = sem("ln_ready")
    mix_held = sem("mix_held")
    mix_root = sem("mix_root")
    mix_sq = sem("mix_sq")
    mix_summed = sem("mix_summed")
    mm_exp = sem("mm_exp")
    mm_ready = sem("mm_ready")
    nm_ready = sem("nm_ready")
    nt_done = sem("nt_done")
    o_copied = sem("o_copied")
    o_done = sem("o_done")
    ones_set = sem("ones_set")
    outputs_written = sem("outputs_written")
    pm_ready = sem("pm_ready")
    post_even = sem("post_even")
    post_odd = sem("post_odd")
    prod1_ready = sem("prod1_ready")
    prod1_used = sem("prod1_used")
    q_rows_copied = sem("q_rows_copied")
    q_rows_done = sem("q_rows_done")
    qb_copied = sem("qb_copied")
    qb_done = sem("qb_done")
    r_ready = sem("r_ready")
    root_ready = sem("root_ready")
    rows_loaded = sem("rows_loaded")
    rsel_ready = sem("rsel_ready")
    s0_loaded = sem("s0_loaded")
    sample_in = sem("sample_in")
    sample_o = sem("sample_o")
    sbias_loaded = sem("sbias_loaded")
    sc_done = sem("sc_done")
    sc_used = sem("sc_used")
    scratch_written = sem("scratch_written")
    silu_ready = sem("silu_ready")
    smb_done = sem("smb_done")
    smexp_ready = sem("smexp_ready")
    smt_done = sem("smt_done")
    smx_ready = sem("smx_ready")
    smz_done = sem("smz_done")
    smzp_done = sem("smzp_done")
    sn_ready = sem("sn_ready")
    snm_ready = sem("snm_ready")
    soft_done = sem("soft_done")
    sp_ln = sem("sp_ln")
    spc_ready = sem("spc_ready")
    sq_ready = sem("sq_ready")
    sq_summed = sem("sq_summed")
    sqrt_ready = sem("sqrt_ready")
    ssum_ready = sem("ssum_ready")
    st_first = sem("st_first")
    st_ready = sem("st_ready")
    tab_loaded = sem("tab_loaded")
    tb0_loaded = sem("tb0_loaded")
    th_ready = sem("th_ready")
    tiles_done = sem("tiles_done")
    tr_copied = sem("tr_copied")
    tr_done = sem("tr_done")
    u_done = sem("u_done")
    u_hi_ready = sem("u_hi_ready")
    u_lo_ready = sem("u_lo_ready")
    uf_ready = sem("uf_ready")
    v_used = sem("v_used")
    vec_ready = sem("vec_ready")
    w_hi_ready = sem("w_hi_ready")
    w_lo_ready = sem("w_lo_ready")
    wa2_loaded = sem("wa2_loaded")
    x_even = sem("x_even")
    x_loaded = sem("x_loaded")
    x_odd = sem("x_odd")
    xc_ready = sem("xc_ready")
    xrows_done = sem("xrows_done")
    xt_copied_even = sem("xt_copied_even")
    xt_copied_odd = sem("xt_copied_odd")
    xt_done = sem("xt_done")
    yt_copied = sem("yt_copied")
    yt_done = sem("yt_done")
    raw_loaded = [sem(f"raw_loaded{i}") for i in range(2)]
    banks_free = [sem(f"banks_free{i}") for i in range(2)]
    kv_loaded = [sem(f"kv_loaded{i}") for i in range(4)]
    k_sent = [sem(f"k_sent{i}") for i in range(2)]
    y_sent = [sem(f"y_sent{i}") for i in range(2)]
    N_OUT = 16
    scratch = nc.dram_tensor("bias_scratch", [HEADS, GREV], F32, kind="Internal").ap()

    def x_first_ready(eng, kt):
        if kt == 0 or eng is nc.vector:
            eng.wait_ge(vec_ready, 1)
            eng.wait_ge(xt_copied_even, 4)
            eng.wait_ge(xt_copied_odd, 4)

    def x_ready(i):
        def ready(eng, kt):
            eng.wait_ge(x_odd if kt % 2 else x_even, 4 * i + kt // 2 + 1)
        return ready

    def input_gate(ve, kt):
        ve.wait_ge(i_ready, kt + 1)
        nc.vector.tensor_tensor(INP[:, kt], TMP[:, kt % 2], XC[:, kt % 2], ALU.mult).then_inc(ix_ready, 1)

    def stage_dram(w, row, col):
        return w.rearrange("(r p) n -> p r n", p=P)[:, row // P:row // P + KT, col]

    def uses(i):
        if i < 32:
            return "k", 0, i
        if i < 96:
            return ("v", 0, (i - 32) // 2) if i % 2 == 0 else ("k", 1, (i - 33) // 2)
        return "v", 1, i - 96

    def place(kind, n):
        if kind == "k":
            return n if n < 32 else 33 + 2 * (n - 32)
        return 32 + 2 * n if n < 32 else 64 + n

    LOADS = 128
    UNITS = [(h, qb) for h in range(HEADS) for qb in range(4)]
    GLA_UNITS = [(tb, hp) for tb in range(4) for hp in range(2)]
    halves = [slice(0, HALF), slice(HALF, T)]

    def banks(par):
        return PS[:, 2 * par:2 * par + 2, 0:HALF]

    def pair(ap):
        return ap.rearrange("p (s t) -> p s t", s=2)

    ctx.enter_context(nc.allow_non_contiguous_dma(reason="vectors and transposed states"))
    block = ctx.enter_context(nc.Block())

    @block.sync
    def _(sp):
        def load(ch, src):
            if ch.static >= 2:
                sp.wait_ge(w_lo_ready, ch.slot_free)
            sp.dma_start(RAW[:, ch.slot], src).then_inc(raw_loaded[ch.slot], 16)

        w_in = a["w_in_even"][0]
        for c in range(IN_CHUNKS):
            col = 256 * c if c < 10 else 2576 + 256 * (c - 10) if c < 12 else 2560
            load(Chunk(c), stage_dram(w_in, 0, slice(col, col + 256)))
        for j in range(4):
            load(Chunk(C_OUT0 + j), stage_dram(a["w_out_even"][0], 0, slice(256 * j, 256 * j + 256)))

        def mlp(layer, c0):
            up = a["w_up"][layer].rearrange("(r p) n -> p r n", p=P)
            down = a["w_down"][layer].rearrange("(q r p) n -> p q r n", p=P, r=KT)
            with sp.Fori(0, 4) as g:
                for j in range(4):
                    load(Chunk(c0 + j, g), up[:, :, bass.ds(g * 1024 + 256 * j, 256)])
                for j in range(4):
                    load(Chunk(c0 + 4 + j, g), down[:, bass.ds(g, 1), :, 256 * j:256 * j + 256]
                         .rearrange("p q r n -> p (q r) n"))

        mlp(0, C_MLP0)
        for j in range(8):
            load(Chunk(C_IN1 + j), stage_dram(a["w_in_odd"][0], 0, slice(256 * j, 256 * j + 256)))
        for j in range(4):
            load(Chunk(C_OUT1 + j), stage_dram(a["w_out_odd"][0], 0, slice(256 * j, 256 * j + 256)))
        mlp(1, C_MLP1)
        load(Chunk(N_CHUNKS), stage_dram(a["w_out_odd"][0], 0, slice(0, 256)))
        for sent in k_sent:
            sp.wait_ge(sent, 32)
        sp.wait_ge(outputs_written, 16 * N_OUT)

    @block.gpsimd
    def _(po):
        po.wait_ge(cidx_ready, 2)

        def pool_product(n):
            i = place("k", n)
            po.wait_ge(kv_loaded[i % 4], 16 * (i // 4 + 1))
            if n == 0:
                po.wait_ge(qb_copied, 2)
            if n >= 1:
                po.wait_ge(prod1_used, n)
            nc.gpsimd.tensor_tensor(PROD[:, 1], KV[:, i % 4, 2:4, :], QB[:, None, n // 32, :].to_broadcast([P, 2, 512]),
                                    ALU.mult).then_inc(prod1_ready, 1)

        def probabilities(b):
            if b >= 2:
                po.wait_ge(v_used, 4 * (b - 1))
            g, pos = b // 8, 16 * (b % 8)
            if b % 8 == 0:
                po.wait_ge(soft_done, 8 * (g + 1))
            nc.gpsimd.tensor_tensor(
                PM[:, b % 2], SC[g][:, :, pos:pos + 16].rearrange("p j n -> p n j")[:, :, None, :].to_broadcast([P, 16, 4, 8]),
                GROUPMASK[:, None, :, None].to_broadcast([P, 16, 4, 8]), ALU.mult).then_inc(pm_ready, 1)

        def release(i):
            kind, g, cc = uses(i)
            n = 32 * g + cc
            if kind == "k":
                pool_product(n)
                po.wait_ge(k_used, n + 1)
                po.wait_ge(prod1_ready, n + 1)
            else:
                if n % 4 == 0:
                    probabilities(n // 4)
                po.wait_ge(v_used, n + 1)

        for i in range(LOADS + 4):
            if i >= 4:
                if i - 4 < LOADS:
                    release(i - 4)
            if i < LOADS:
                kind, g, cc = uses(i)
                po.indirect_dma_start(KV[:, i % 4].rearrange("p n f -> p (n f)"), None, cache[kind],
                                      bass.IndirectOffsetOnAxis(ap=CIDX[g][:], axis=0),
                                      element_offset=cc * 2048).then_inc(kv_loaded[i % 4], 16)

        def post_add(i):
            for kt in range(1, KT, 2):
                po.wait_ge(post_odd, 4 * i + kt // 2 + 1)
                nc.gpsimd.tensor_tensor(X[:, kt], X[:, kt], TMP[:, 1], ALU.add).then_inc(x_odd, 1)
        for i in range(4):
            post_add(i)

    @block.scalar
    def _(act):
        chain = [0]

        def link(ins):
            chain[0] += 1
            ins.then_inc(act_step, 1)
            act.wait_ge(act_step, chain[0])

        A = nc.scalar.activation

        def out_dma(dst, src):
            act.dma_start(dst, src).then_inc(outputs_written, 16)

        act.dma_start(CONST[:], a["consts"][:, 0:C_HOT]).then_inc(const_loaded, 16)
        for tb in range(4):
            act.dma_start(XIN[:, tb], x_in[P * tb:P * tb + P, :]).then_inc(x_loaded, 16)
        act.dma_start(XSIN[:], xs_in).then_inc(x_loaded, 16)
        act.dma_start(PIDX[:], a["page_table"].rearrange("(g b) n -> g (b n)", g=2).rearrange("g p -> p g")
).then_inc(idx_loaded, 16)
        rows = [(VROWS[0:64], a["norm_g"].rearrange("l i (k p) -> (l i k) p", p=P)),
                (VROWS[64:96], a["conv_w"][0].rearrange("j (k p) -> (j k) p", p=P)),
                (VROWS[96:104], a["conv_b"][0].rearrange("(k p) -> k p", p=P)),
                (VROWS[104:112], a["b_gate_a"][0].rearrange("(k p) -> k p", p=P)),
                (VROWS[112:120], a["b_gate_x"][0].rearrange("(k p) -> k p", p=P)),
                (VROWS[120:128], a["rg_lambda"][0].rearrange("(k p) -> k p", p=P)),
                (VROWS2[0:2], a["b_alpha2"][0].rearrange("(k p) -> k p", p=P)),
                (VROWS2[2:3], a["g_diff"]), (VROWS2[3:4], a["g_gla"]),
                (SROWS[0:24], a["state_conv"][0].rearrange("b j d -> (b j) d")),
                (SROWS[24:32], a["state_rglru"][0])]
        for dst, src in rows:
            act.dma_start(dst, src).then_inc(rows_loaded, 16)
        for i, n in enumerate(("lam_q1", "lam_k1", "lam_q2", "lam_k2")):
            act.dma_start(LAMIN[:, i], a[n].to_broadcast([P, DH])).then_inc(lam_loaded, 16)
        act.dma_start(TAB[0:32], a["rel_table"]).then_inc(tab_loaded, 16)
        act.dma_start(HOT[:], a["consts"][0:33, C_HOT:C_HOT + GREV]).then_inc(tab_loaded, 16)
        act.dma_start(TB0[:], a["rel_table"][0:1, :].to_broadcast([P, 4])).then_inc(tb0_loaded, 16)
        act.dma_start(WA2[:], a["w_alpha2"][0]).then_inc(wa2_loaded, 16)

        for i in range(4):
            act.wait_ge(xt_done, 2 * i + 2)
            A(X[:, 2 * i + 1, 0:SEQ], PS[:, (2 * i + 1) % 4], ACT.Copy).then_inc(xt_copied_odd, 1)
        act.wait_ge(lam_sums, 1)
        A(LAM[:, 0:2], LAM[:, 0:2], ACT.Exp).then_inc(lam_exp, 1)
        act.wait_ge(g_done, 1)
        A(GSB[:, 0:512], PS[0:4, 7, :], ACT.Copy)
        link(A(GSB[:, 512:GREV], PS[0:4, 6, 256:384], ACT.Copy))
        act.dma_start(scratch, GSB[:]).then_inc(scratch_written, 16)

        def split_hi(ch):
            act.wait_ge(raw_loaded[ch.slot], ch.loaded)
            if ch.static >= 2:
                act.wait_ge(tiles_done, ch.prev_done)
            A(W_hi[:, ch.slot], RAW[:, ch.slot], ACT.Copy).then_inc(w_hi_ready, 1)

        def squares(n, src, ready):
            for kt in range(KT):
                ready(act, kt)
                if 8 * n + kt >= 2:
                    act.wait_ge(sq_summed, 8 * n + kt - 1)
                A(SQ[:, kt % 2], src[:, kt], ACT.Square).then_inc(sq_ready, 1)
            act.wait_ge(sq_summed, 8 * n + 8)
            if n >= 1:
                act.wait_ge(inverse_ready, n)
            A(pair(RS[:, 0]), PS[:, 4:6, 0:HALF], ACT.Sqrt, scale=1.0 / D_MODEL, bias=EPSC[:, 0:1]).then_inc(root_ready, 1)

        def normed_hi(m, before):
            if before:
                act.wait_ge(tiles_done, before)
            for kt in range(KT):
                act.wait_ge(hf_ready, 8 * m + kt + 1)
                A(H_hi[:, kt], TMP[:, kt % 2], ACT.Copy).then_inc(hhi_ready, 1)

        squares(0, X, x_first_ready)
        split_hi(Chunk(0))
        normed_hi(0, 0)
        for c in range(IN_CHUNKS):
            if c + 1 < IN_CHUNKS:
                split_hi(Chunk(c + 1))
            ch = Chunk(c)
            for m, par, done in zip(ch.tiles, ch.par, ch.done):
                if par:
                    continue
                act.wait_ge(tiles_done, done)
                if m == 12:
                    act.wait_ge(scratch_written, 16)
                if m < 24:
                    A(pair(PJ[:, m]), banks(0), ACT.Copy, scale=SCALE if m < 4 or m == 12 else 1.0).then_inc(banks_free[0], 1)
                else:
                    A(pair(LR[0:RANK]), PS[0:RANK, 0:2, 0:HALF], ACT.Copy).then_inc(banks_free[0], 1)
            if c == 3:
                act.wait_ge(q_rows_done, 1)
                A(QTOK[:], PS[0:8, 6, :], ACT.Copy).then_inc(q_rows_copied, 1)

        act.wait_ge(tiles_done, first_tile(C_OUT0))
        act.wait_ge(scratch_written, 16)
        act.dma_start(FLIPPED[:], bass.AP(scratch.tensor, 0, [[1, P], [GREV, HEADS], [1, 512]])).then_inc(bias_loaded, 16)
        act.dma_start(EXCHANGE[:], a["consts"][:, C_EXCH:C_EXCH + P]).then_inc(bias_loaded, 16)
        act.dma_start(SBIAS[:], bass.AP(scratch.tensor, 0, [[0, P], [GREV, HEADS], [1, PAGE]])).then_inc(sbias_loaded, 16)
        act.wait_ge(sbias_loaded, 16)
        for b in range(4):
            row = N_PAGES * (b + 1) - 1
            act.dma_start(SBIAS[row:row + 1], bass.AP(scratch.tensor, 383, [[0, 1], [GREV, HEADS], [1, PAGE]])
                          ).then_inc(sbias_loaded, 16)

        k_out, v_out = o["k_prompt"], o["v_prompt"]
        for i in range(12):
            tb, what = divmod(i, 3)
            act.wait_ge(tr_done, i + 1)
            if what == 0:
                if tb >= 2:
                    act.wait_ge(k_sent[tb % 2], 16)
                dst = KSTAGE[:, tb % 2]
            else:
                dst = (VT, GVT)[what - 1][:, tb]
            A(dst, PS[:, i % 4], ACT.Copy).then_inc(tr_copied, 1)
            if what < 2:
                act.wait_ge(tr_copied, i + 1)
                t = act.dma_start((k_out, v_out)[what][P * tb:P * tb + P, :], dst)
                t.then_inc(k_sent[tb % 2] if what == 0 else outputs_written, 16)
        for i in range(3):
            act.wait_ge(tr_done, 13 + i)
            if i == 2:
                act.wait_ge(sample_in, 1)
            dst = (KVTOK[:, 0:512], KVTOK[:, 512:1024], GVTOK[:])[i]
            A(dst, PS[0:8, i, :], ACT.Copy).then_inc(tr_copied, 1)
            if i < 2:
                act.wait_ge(tr_copied, 13 + i)
                out_dma((o["k_sample"], o["v_sample"])[i], dst)
        for sent in k_sent:
            act.wait_ge(sent, 32)
        act.wait_ge(outputs_written, 16 * 6)
        act.wait_ge(tr_copied, 15)

        act.wait_ge(sample_in, 1)
        for par in range(2):
            act.dma_start(S0[64 * par:64 * par + 64],
                          a["state_gla"][0].rearrange("b (hp q) k v -> q k b hp v", q=2)[par]).then_inc(s0_loaded, 16)
        act.wait_ge(flip_done, HEADS)
        A(BIAS[:], PS[:, 4:8, :], ACT.Copy).then_inc(bias_ready, 1)
        for hp in range(2):
            act.wait_ge(la_done, hp + 1)
            if hp:
                act.wait_ge(kd_ready, 1)
            link(A(pair(XL[:, 0]), PS[:, 4 + 2 * hp:6 + 2 * hp, 0:HALF], ACT.Identity, bias=VEC2[:, hp:hp + 1]))
            link(A(XL[:, 1], XL[:, 0], ACT.Abs))
            link(A(XL[:, 1], XL[:, 1], ACT.Exp, scale=-1.0))
            A(XL[:, 1], XL[:, 1], ACT.Ln, bias=1.0).then_inc(ln_ready, 1)
            act.wait_ge(bc_ready, hp + 1)
            A(XL[:, 0, 0:SEQ], BC[:, hp], ACT.Exp)
            A(XL[:, 1, 0:SEQ], BC[:, hp], ACT.Exp, scale=-1.0)
            A(DECC[:, hp], BC[:, hp, GLA_CHUNK - 1::GLA_CHUNK], ACT.Exp)
            A(EAS[:, hp], LAS[:, hp], ACT.Exp)
            A(ENS[:, hp], LAS[:, hp], ACT.Exp, scale=-1.0).then_inc(eb_ready, 1)
            act.wait_ge(kdx_ready, hp + 1)
            A(XL[:, 2, 0:SEQ], XL[:, 2, 0:SEQ], ACT.Exp).then_inc(kdx_exp, 1)

        for u, (h, qb) in enumerate(UNITS):
            n = P * (qb + 1)
            act.wait_ge(nm_ready, u + 1)
            for c in range(2):
                t = A(PR[:, c, 0:n], PR[:, c, 0:n], ACT.Exp, bias=NM[:, c:c + 1], accum_out=SM[:, c:c + 1])
            t.then_inc(ex_done, 1)
            act.wait_ge(at_done, u + 1)
            A(AT[:, 0:n], PS[:, 2, 0:n], ACT.Copy).then_inc(at_copied, 1)
            act.wait_ge(o_done, u + 1)
            A(PJ[:, h, P * qb:P * qb + P], PS[:, 3, 0:P], ACT.Copy).then_inc(o_copied, 1)

        def softmax(g):
            act.wait_ge(snm_ready, g + 1)
            for j in range(8):
                A(SC[g][:, j], SC[g][:, j], ACT.Exp, bias=NROW[:, j:j + 1], accum_out=ROWSUM[:, j:j + 1]).then_inc(soft_done, 1)

        softmax(0)
        for u, (tb, hp) in enumerate(GLA_UNITS):
            for par in range(2):
                act.wait_ge(go_done, 2 * u + par + 1)
                A(PJ[:, 4 + 2 * hp + par, P * tb:P * tb + P], PS[:, 2 + par, 0:P], ACT.Copy).then_inc(go_copied, 1)
        softmax(1)
        act.wait_ge(st_ready, 64)
        act.wait_ge(gs_v_used, N_SAMPLE)
        for hp in range(2):
            out_dma(o["gla_prompt"][hp], ST[:, hp, 8])
        for par in range(2):
            out_dma(o["gla_sample"].rearrange("b (hp q) k v -> q k b hp v", q=2)[par], S0[64 * par:64 * par + 64])

        act.wait_ge(v_used, 64)
        for i, n in enumerate(("w_gate_a", "w_gate_x")):
            act.dma_start(WG[i][:], a[n][0].rearrange("n d e -> d n e")).then_inc(gates_loaded, 16)

        act.wait_ge(mm_ready, 1)
        A(E1[:], E1[:], ACT.Exp)
        A(E2[:], E2[:], ACT.Exp).then_inc(mm_exp, 1)

        for t in range(4):
            A(PJ[:, 20 + t], PJ[:, 20 + t], ACT.Silu).then_inc(silu_ready, 1)
        act.wait_ge(outputs_written, 16 * 10)
        for t in range(KT + 2):
            if t < KT:
                act.wait_ge(mix_held, t + 1)
                A(SQ[:, t % 2], SQ[:, t % 2], ACT.Square, scale=2.0 ** -4).then_inc(mix_sq, 1)
            if 1 <= t <= KT:
                q = t - 1
                act.wait_ge(mix_summed, q + 1)
                if q >= 2:
                    act.wait_ge(hf_ready, 8 + q - 1)
                A(pair(RS[:, q % 2]), PS[:, 4 + 2 * (q % 2):6 + 2 * (q % 2), 0:HALF], ACT.Sqrt, scale=2.0 ** -9,
                  bias=EPSC[:, 1:2]).then_inc(mix_root, 1)
            if t >= 2:
                q = t - 2
                act.wait_ge(hf_ready, 8 + q + 1)
                A(H_hi[:, q], TMP[:, q % 2], ACT.Copy).then_inc(hhi_ready, 1)
        split_hi(Chunk(C_OUT0))

        def copies(c0, dst):
            for j in range(4 if dst is ACC else 8):
                ch = Chunk(c0 + j)
                split_hi(Chunk(c0 + j + 1))
                for i in range(2):
                    if ch.par[i] == 0:
                        act.wait_ge(tiles_done, ch.done[i])
                        A(pair(dst[:, 2 * j + i]), banks(0), ACT.Copy).then_inc(banks_free[0], 1)

        def mlp(layer, c0):
            with act.Fori(0, 4) as g:
                for j in range(8):
                    split_hi(Chunk(c0 + j + 1, g))
                    if j < 4:
                        ch = Chunk(c0 + j, g)
                        for i in range(2):
                            u = 2 * j + i
                            act.wait_ge(tiles_done, ch.done[i])
                            if u >= 2:
                                act.wait_ge(u_lo_ready, g * 8 + (32 * layer + u - 1))
                            A(pair(RL[:, i]), banks(ch.par[i]), ACT.Relu).then_inc(banks_free[ch.par[i]], 1)
                            act.wait_ge(banks_free[ch.par[i]], ch.banks_free[i] + 1)
                            A(UF[:, i], RL[:, i], ACT.Square).then_inc(uf_ready, 1)

        def acc_ready(c0):
            def ready(eng, kt):
                m = first_tile(c0) + kt
                eng.wait_ge(banks_free[m % 2], m // 2 + 1)
            return ready

        copies(C_OUT0, ACC)
        squares(1, ACC, acc_ready(C_OUT0))
        squares(2, X, x_ready(0))
        normed_hi(2, first_tile(C_MLP0))
        mlp(0, C_MLP0)
        squares(3, ACC, acc_ready(C_IN1 - 4))
        squares(4, X, x_ready(1))
        normed_hi(3, first_tile(C_IN1))
        copies(C_IN1, GX)

        act.dma_start(o["conv_sample"][:, 0:2, :], a["state_conv"][0][:, 1:3, :]).then_inc(outputs_written, 16)
        act.wait_ge(xrows_done, 1)
        link(A(STOK[:].rearrange("t (b n) -> t b n", b=2), PS[0:11, 6:8, :], ACT.Copy))
        out_dma(o["conv_prompt"], STOK[0:3])
        out_dma(o["conv_sample"][:, 2, :], STOK[3:11])
        link(A(SPT[:, 0], VEC[:, V_LAM:V_LAM + KT], ACT.Abs))
        link(A(SPT[:, 0], SPT[:, 0], ACT.Exp, scale=-1.0))
        A(SPT[:, 0], SPT[:, 0], ACT.Ln, bias=1.0).then_inc(sp_ln, 1)
        for kt in range(KT):
            act.wait_ge(gates_done, kt + 1)
            A(pair(RG[:, kt]), banks(0), ACT.Sigmoid, bias=VEC[:, V_BA + kt:V_BA + kt + 1]).then_inc(r_ready, 1)
            if kt >= 2:
                act.wait_ge(ix_ready, kt - 1)
            A(pair(TMP[:, kt % 2]), banks(1), ACT.Sigmoid, bias=VEC[:, V_BX + kt:V_BX + kt + 1]).then_inc(i_ready, 1)
        act.wait_ge(spc_ready, 1)
        act.wait_ge(r_ready, KT)
        for kt in range(KT):
            A(DEC[:, kt], RG[:, kt], ACT.Exp, scale=SPC[:, kt:kt + 1])
            A(RG[:, kt], RG[:, kt], ACT.Tanh, scale=SPC[:, kt:kt + 1]).then_inc(th_ready, 1)
        for kt in range(KT):
            act.wait_ge(em_ready, kt + 1)
            A(RG[:, kt], RG[:, kt], ACT.Sqrt).then_inc(sqrt_ready, 1)
        for kt in range(KT):
            A(GX[:, kt], GX[:, kt], ACT.Gelu_apprx_tanh).then_inc(gelu_ready, 1)
        act.wait_ge(tiles_done, first_tile(C_OUT1))
        for kt in range(KT):
            act.wait_ge(hf_ready, 32 + kt + 1)
            A(H_hi[:, kt], TMP[:, kt % 2], ACT.Copy).then_inc(hhi_ready, 1)
        act.wait_ge(hrows_done, 1)
        act.wait_ge(outputs_written, 16 * 13)
        A(HTOK[0:9].rearrange("t (b n) -> t b n", b=2), PS[0:9, 4:6, :], ACT.Copy).then_inc(hrows_copied, 1)
        act.wait_ge(hrows_copied, 1)
        out_dma(o["rglru_prompt"], HTOK[0:1])
        out_dma(o["rglru_sample"], HTOK[1:9])

        copies(C_OUT1, ACC)
        squares(5, ACC, acc_ready(C_OUT1))
        squares(6, X, x_ready(2))
        normed_hi(5, first_tile(C_MLP1))
        mlp(1, C_MLP1)
        squares(7, ACC, acc_ready(N_CHUNKS - 4))
        for tb in range(4):
            act.wait_ge(yt_done, tb + 1)
            if tb >= 2:
                act.wait_ge(y_sent[tb % 2], 16)
            A(YT[:, tb % 2].rearrange("t (b n) -> t b n", b=2), PS[:, 2 * (tb % 2):2 * (tb % 2) + 2, :], ACT.Copy).then_inc(yt_copied, 1)
            act.wait_ge(yt_copied, tb + 1)
            act.dma_start(o["y_prompt"][P * tb:P * tb + P, :], YT[:, tb % 2]).then_inc(y_sent[tb % 2], 16)
        act.wait_ge(yt_done, 5)
        link(A(YS[:].rearrange("t (b n) -> t b n", b=2), PS[0:8, 4:6, :], ACT.Copy))
        out_dma(o["y_sample"], YS[:])
        act.wait_ge(y_sent[0], 32)
        act.wait_ge(y_sent[1], 32)

    @block.vector
    def _(ve):
        chain = [0]

        def link(ins):
            chain[0] += 1
            ins.then_inc(dve_step, 1)
            ve.wait_ge(dve_step, chain[0])

        V = nc.vector
        V.memset(ONES[:], 1.0)
        V.memset(EPSC[:, 0:1], EPS)
        V.memset(EPSC[:, 1:2], EPS / 1024)
        V.memset(TAB[32:33], NEG).then_inc(ones_set, 1)
        ve.wait_ge(idx_loaded, 16)
        for g in range(2):
            V.tensor_scalar(CIDX[g][:], PIDX[:, g:g + 1], 32, None, ALU.mult).then_inc(cidx_ready, 1)

        for i in range(4):
            ve.wait_ge(xt_done, 2 * i + 1)
            V.tensor_copy(X[:, 2 * i, 0:SEQ], PS[:, (2 * i) % 4]).then_inc(xt_copied_even, 1)
        ve.wait_ge(xt_done, 9)
        V.tensor_copy(X[:, :, SEQ:T], PS[:, 4, 0:8 * KT].rearrange("p (k b) -> p k b", k=KT))
        V.tensor_copy(VEC[:], PS[:, 5, 0:P])
        V.tensor_copy(VEC2[:], PS[:, 5, P:P + 4])
        V.tensor_copy(STATE[:], PS[:, 6, 0:256].rearrange("p (k r) -> p k r", k=KT)).then_inc(vec_ready, 1)
        ve.wait_ge(lam_loaded, 64)
        lam_in = LAMIN[:].rearrange("p (a two) d -> p a two d", two=2)
        link(V.tensor_tensor(LAMPR[:], lam_in[:, :, 0], lam_in[:, :, 1], ALU.mult))
        V.tensor_reduce(LAM[:, 0:2], LAMPR[:], AX.X, ALU.add).then_inc(lam_sums, 1)

        def split_lo(ch):
            ve.wait_ge(w_hi_ready, ch.ready)
            V.tensor_tensor(W_lo[:, ch.slot], RAW[:, ch.slot], W_hi[:, ch.slot].bitcast(F32), ALU.subtract).then_inc(w_lo_ready, 1)

        def set_lo(m, kt):
            ve.wait_ge(hhi_ready, 8 * m + kt + 1)
            V.tensor_tensor(H_lo[:, kt], TMP[:, kt % 2], H_hi[:, kt].bitcast(F32), ALU.subtract).then_inc(h_ready, 1)

        def root(n):
            ve.wait_ge(root_ready, n + 1)
            V.reciprocal(RS[:, 1], RS[:, 0]).then_inc(inverse_ready, 1)
            ve.wait_ge(inverse_ready, n + 1)

        def normed(n, m, gain):
            root(n)
            for kt in range(KT + 1):
                if kt < KT:
                    if kt >= 2:
                        ve.wait_ge(h_ready, 8 * m + kt - 1)
                    t = V.scalar_tensor_tensor(TMP[:, kt % 2], X[:, kt], VEC[:, gain + kt:gain + kt + 1], RS[:, 1], ALU.mult, ALU.mult)
                    t.then_inc(hf_ready, 1)
                if kt >= 1:
                    set_lo(m, kt - 1)

        def post(n, i, gain):
            root(n)
            for kt in range(0, KT, 2):
                for q in range(2):
                    if kt >= 2:
                        ve.wait_ge(x_odd if q else x_even, 4 * i + kt // 2)
                    t = V.scalar_tensor_tensor(TMP[:, q], ACC[:, kt + q], VEC[:, gain + kt + q:gain + kt + q + 1], RS[:, 1], ALU.mult, ALU.mult)
                    t.then_inc(post_odd if q else post_even, 1)
                ve.wait_ge(post_even, 4 * i + kt // 2 + 1)
                V.tensor_tensor(X[:, kt], X[:, kt], TMP[:, 0], ALU.add).then_inc(x_even, 1)

        k_done = [0]

        def k_chunks(count):
            for n in range(k_done[0], k_done[0] + count):
                g, i = n // 32, place("k", n)
                pos = 4 * (n % 32)
                ve.wait_ge(kv_loaded[i % 4], 16 * (i // 4 + 1))
                V.tensor_tensor(PROD[:, 0], KV[:, i % 4, 0:2, :], QB[:, None, g, :].to_broadcast([P, 2, 512]), ALU.mult).then_inc(k_used, 1)
                ve.wait_ge(k_used, n + 1)
                for half in range(2):
                    if half:
                        ve.wait_ge(prod1_ready, n + 1)
                    out = SC[g][:, :, pos + 2 * half:pos + 2 * half + 2].rearrange("p j n -> p n j")
                    t = V.tensor_reduce(out, PROD[:, half].rearrange("p n (j d) -> p n j d", d=DH), AX.X, ALU.add)
                    if half:
                        t.then_inc(prod1_used, 1)
                    else:
                        link(t)
            k_done[0] += count

        ve.wait_ge(vec_ready, 1)
        root(0)
        x_first_ready(ve, KT - 1)
        for kt in range(KT + 1):
            if kt < KT:
                if kt >= 2:
                    ve.wait_ge(h_ready, kt - 1)
                V.scalar_tensor_tensor(TMP[:, kt % 2], X[:, kt], VEC[:, kt:kt + 1], RS[:, 1], ALU.mult, ALU.mult).then_inc(hf_ready, 1)
            if kt >= 1:
                set_lo(0, kt - 1)
            if kt == KT:
                split_lo(Chunk(0))
        ve.wait_ge(lam_exp, 1)
        link(V.tensor_scalar(LAM[:, 3:4], LAM[:, 1:2], -LAM_INIT, None, ALU.add))
        V.tensor_tensor(LAM[:, 2:3], LAM[:, 3:4], LAM[:, 0:1], ALU.subtract)
        V.tensor_scalar(GD8[:], VEC2[:, 2:3], 1.0 - LAM_INIT, None, ALU.mult)
        for c in range(IN_CHUNKS):
            if c + 1 < IN_CHUNKS:
                split_lo(Chunk(c + 1))
            ch = Chunk(c)
            for m, par, done in zip(ch.tiles, ch.par, ch.done):
                if not par:
                    continue
                ve.wait_ge(tiles_done, done)
                if m == 13:
                    ve.wait_ge(scratch_written, 16)
                V.tensor_scalar(pair(PJ[:, m]), banks(1), SCALE if m < 4 or m == 13 else 1.0, None, ALU.mult).then_inc(banks_free[1], 1)
            if c == 3:
                ve.wait_ge(qb_done, 1)
                V.tensor_copy(QB[:, 0], PS[:, 6, :]).then_inc(qb_copied, 1)
                ve.wait_ge(qb_done, 2)
                V.tensor_copy(QB[:, 1], PS[:, 7, :]).then_inc(qb_copied, 1)
                ve.wait_ge(qb_copied, 2)
            if c >= 4:
                k_chunks(2)

        ve.wait_ge(banks_free[0], 12)
        ve.wait_ge(banks_free[1], 12)
        V.tensor_tensor(QKP[:], PJ[:, 0:4, SEQ:T], PJ[:, 4:8, SEQ:T], ALU.mult)
        V.tensor_copy(VSC[:], PJ[:, 8:12, SEQ:T])
        V.tensor_copy(GVC[:], PJ[:, 16:20, SEQ:T]).then_inc(sample_in, 1)
        ve.wait_ge(sample_in, 1)
        ve.wait_ge(tr_done, 15)
        V.tensor_copy(RSEL[:], IDENT[0:8, 0:8, None].to_broadcast([8, 8, P])).then_inc(rsel_ready, 1)
        link(V.memset(SCANM[:], 1.0))
        link(V.memset(SCANM[:, 0::GLA_CHUNK], 0.0))

        for hp in range(2):
            ve.wait_ge(ln_ready, hp + 1)
            link(V.tensor_scalar(XL[:, 2], XL[:, 0], 0.0, None, ALU.min))
            link(V.tensor_tensor(XL[:, 2], XL[:, 2], XL[:, 1], ALU.subtract))
            link(V.tensor_scalar(XL[:, 2], XL[:, 2], 1.0 / GLA_TAU, None, ALU.mult))
            V.tensor_copy(LAS[:, hp], XL[:, 2, SEQ:T])
            V.tensor_tensor_scan(BC[:, hp], SCANM[:], XL[:, 2, 0:SEQ], 0.0, ALU.mult, ALU.add).then_inc(bc_ready, 1)
            ve.wait_ge(bc_ready, hp + 1)
            by_chunk = BC[:, hp].rearrange("p (n c) -> p n c", c=GLA_CHUNK)
            V.tensor_tensor(XL[:, 2, 0:SEQ].rearrange("p (n c) -> p n c", c=GLA_CHUNK),
                            by_chunk[:, :, GLA_CHUNK - 1:GLA_CHUNK].to_broadcast([P, SEQ // GLA_CHUNK, GLA_CHUNK]),
                            by_chunk, ALU.subtract).then_inc(kdx_ready, 1)
            ve.wait_ge(eb_ready, hp + 1)
            V.tensor_tensor(QE[:, hp], PJ[:, 12 + hp, 0:SEQ], XL[:, 0, 0:SEQ], ALU.mult)
            V.tensor_tensor(KE[:, hp], PJ[:, 14 + hp, 0:SEQ], XL[:, 1, 0:SEQ], ALU.mult)
            V.tensor_tensor(QES[:, hp], PJ[:, 12 + hp, SEQ:T], EAS[:, hp], ALU.mult)
            V.tensor_tensor(KES[:, hp], PJ[:, 14 + hp, SEQ:T], ENS[:, hp], ALU.mult)
            link(V.tensor_copy(KSS[:, hp], PJ[:, 14 + hp, SEQ:T]))
            V.tensor_tensor(AKS[:, hp], QES[:, hp], KES[:, hp], ALU.mult)
            ve.wait_ge(kdx_exp, hp + 1)
            V.tensor_tensor(KD[:, hp], PJ[:, 14 + hp, 0:SEQ], XL[:, 2, 0:SEQ], ALU.mult).then_inc(kd_ready, 1)
        V.memset(ST[:, :, 0], 0.0).then_inc(st_first, 1)
        V.memset(ATTM[:], 0.0).then_inc(st_first, 1)
        ve.wait_ge(st_first, 2)

        ve.wait_ge(tb0_loaded, 16)
        ve.wait_ge(nt_done, 1)
        for c in range(2):
            V.tensor_tensor(SN[:].rearrange("p b h c -> p c h b")[:, c], PS[:, 4 + c, 0:32].rearrange("p (h b) -> p h b", h=4),
                            TB0[:, :, None].to_broadcast([P, 4, 8]), ALU.add).then_inc(sn_ready, 1)
        ve.wait_ge(gs_done, 1)
        gv, os_ = GVC[:].rearrange("p (hp q) b -> p q hp b", q=2), OS[:].rearrange("p (hp q) b -> p q hp b", q=2)
        go = PJ[:, 4:8, SEQ:T].rearrange("p (hp q) b -> p q hp b", q=2)
        for par in range(2):
            t = V.tensor_tensor(os_[:, par], gv[:, par], PS[:, par, 0:16].rearrange("p (h b) -> p h b", h=2), ALU.mult)
        link(t)
        for par in range(2):
            V.tensor_tensor(go[:, par], os_[:, par], PS[:, 2 + par, 0:16].rearrange("p (h b) -> p h b", h=2), ALU.add).then_inc(go_s_ready, 1)
        ve.wait_ge(s0_loaded, 32)
        link(V.tensor_tensor(S0[:], S0[:], EAS[:].rearrange("p h b -> p b h")[:, :, :, None].to_broadcast([P, 8, 2, P]), ALU.mult))
        for b in range(N_SAMPLE):
            ve.wait_ge(gs_v_done, b + 1)
            for h in range(HEADS):
                hp, rows = h // 2, slice(64 * (h % 2), 64 * (h % 2) + 64)
                t = V.scalar_tensor_tensor(S0[rows, b, hp], PS[rows, 4 + b % 2, P * h:P * h + P], KSS[rows, hp, b:b + 1],
                                           S0[rows, b, hp], ALU.mult, ALU.add)
            t.then_inc(gs_v_used, 1)

        ve.wait_ge(bias_ready, 1)
        for sent in k_sent:
            ve.wait_ge(sent, 32)
        for u, (h, qb) in enumerate(UNITS):
            n = P * (qb + 1)
            ve.wait_ge(sc_done, u + 1)
            if u:
                ve.wait_ge(ad_ready, u)
            for c in range(2):
                t = V.tensor_tensor(PR[:, c, 0:n], PS[:, c, 0:n], BIAS[:, h, 512 - n:512], ALU.add)
            t.then_inc(sc_used, 1)
            ve.wait_ge(sc_used, u + 1)
            link(V.tensor_reduce(MX[:], PR[:, :, 0:n], AX.X, ALU.max))
            V.tensor_scalar(NM[:], MX[:], -1.0, None, ALU.mult).then_inc(nm_ready, 1)
            k_chunks(1 if k_done[0] < 32 else 0)
            ve.wait_ge(ex_done, u + 1)
            link(V.reciprocal(RR[:], SM[:]))
            link(V.tensor_tensor(RR[:, 1:2], RR[:, 1:2], LAM[:, 2:3], ALU.mult))
            if u:
                ve.wait_ge(at_done, u)
            link(V.tensor_scalar(AD[:, 0:n], PR[:, 0, 0:n], RR[:, 0:1], None, ALU.mult))
            V.scalar_tensor_tensor(AD[:, 0:n], PR[:, 1, 0:n], RR[:, 1:2], AD[:, 0:n], ALU.mult, ALU.add).then_inc(ad_ready, 1)
        assert k_done[0] == 32

        def softmax(g):
            ve.wait_ge(sbias_loaded, 80)
            ve.wait_ge(prod1_used, k_done[0])
            by_head = SC[g][:].rearrange("p (h c) n -> p h c n", c=2)
            if g:
                ve.wait_ge(smzp_done, 1)
            for c in range(2):
                t = V.tensor_tensor(by_head[:, :, c], by_head[:, :, c], SBIAS[:], ALU.add)
            link(t)
            V.tensor_reduce(ROWMX[:], SC[g][:], AX.X, ALU.max).then_inc(smx_ready, 1)
            ve.wait_ge(smt_done, g + 1)
            link(V.tensor_reduce(M84[:], PS[0:8, 6, 0:P].rearrange("p (b n) -> p b n", b=4), AX.X, ALU.max))
            V.tensor_copy(MEXP[:], M84[:, :, None].to_broadcast([8, 4, 32]))
            V.tensor_tensor(MDIAG[:], M84[:, :, None].to_broadcast([8, 4, 8]),
                            IDENT[0:8, None, 0:8].to_broadcast([8, 4, 8]), ALU.mult).then_inc(smexp_ready, 1)
            ve.wait_ge(smb_done, g + 1)
            V.tensor_scalar(NROW[:], PS[:, 6, 128:136], -1.0, None, ALU.mult).then_inc(snm_ready, 1)
            V.tensor_copy(MP[:, g], PS[:, 6, 256:288].rearrange("p (b j) -> p b j", b=4))
            ve.wait_ge(soft_done, 8 * (g + 1))
            V.tensor_tensor(ZS[:], ROWSUM[:, None, :].to_broadcast([P, 4, 8]), GROUPMASK[:, :, None].to_broadcast([P, 4, 8]),
                            ALU.mult).then_inc(ssum_ready, 1)
            ve.wait_ge(smz_done, g + 1)
            V.tensor_copy(ZP[:, g], PS[:, 6, 288:320].rearrange("p (b j) -> p b j", b=4)).then_inc(smzp_done, 1)

        softmax(0)
        for u, (tb, hp) in enumerate(GLA_UNITS):
            k_chunks(4)
            ve.wait_ge(kdt_done, u + 1)
            if u:
                ve.wait_ge(u_done, u)
            V.tensor_tensor(KDM[:], PS[:, 6, None, 384:512].to_broadcast([P, 8, P]),
                            CHUNKMASK[:, :, None].to_broadcast([P, 8, P]), ALU.mult).then_inc(kdm_ready, 1)
            for par in range(2):
                ve.wait_ge(att_done, 2 * u + par + 1)
                if u:
                    ve.wait_ge(go_done, 2 * (u - 1) + par + 1)
                V.copy_predicated(ATTM[:, par], ATTMASK, PS[:, par, 0:P]).then_inc(attm_ready, 1)
            if tb:
                V.tensor_copy(ST[:, hp, 0], ST[:, hp, 8]).then_inc(st_first, 1)
                ve.wait_ge(st_first, u + 1)
            ve.wait_ge(u_done, u + 1)
            for n in range(8):
                V.scalar_tensor_tensor(ST[:, hp, n + 1], ST[:, hp, n], DECC[:, hp, 8 * tb + n:8 * tb + n + 1],
                                       PS[:, 4 + n // 4, P * (n % 4):P * (n % 4) + P], ALU.mult, ALU.add).then_inc(st_ready, 1)
                ve.wait_ge(st_ready, 8 * u + n + 1)
        softmax(1)

        mp, zp, sn = (t.rearrange(r) for t, r in ((MP[:], "p g b j -> p (g b j)"), (ZP[:], "p g b j -> p (g b j)"),
                                                  (SN[:], "p b h c -> p (b h c)")))
        ve.wait_ge(smzp_done, 2)
        link(V.tensor_tensor(MM[:], mp, sn, ALU.max))
        V.tensor_tensor(E1[:], mp, MM[:], ALU.subtract)
        V.tensor_tensor(E2[:], sn, MM[:], ALU.subtract).then_inc(mm_ready, 1)
        ve.wait_ge(mm_exp, 1)
        link(V.tensor_tensor(ZZ[:], zp, E1[:], ALU.mult))
        link(V.tensor_tensor(ZZ[:], ZZ[:], E2[:], ALU.add))
        link(V.reciprocal(ZZ[:], ZZ[:]))
        parts = lambda t: t[:].rearrange("p (b h c) -> p c h b", h=4, c=2)
        z1 = ZZ[:].rearrange("p (x c) -> p c x", c=2)[:, 1]
        link(V.tensor_scalar(z1, z1, LAM[:, 2:3], None, ALU.mult))
        V.tensor_tensor(E1[:], E1[:], ZZ[:], ALU.mult)
        link(V.tensor_tensor(E2[:], E2[:], ZZ[:], ALU.mult))
        ve.wait_ge(v_used, 64)
        for c in range(2):
            for g in range(2):
                t = V.tensor_tensor(OW[:, c, :, 4 * g:4 * g + 4],
                                    PS[:, 7, 32 * g:32 * g + 32].rearrange("p (h b c) -> p c h b", h=4, c=2)[:, c],
                                    parts(E1)[:, c, :, 4 * g:4 * g + 4], ALU.mult)
        link(V.tensor_tensor(OS[:], parts(E2)[:, 0], parts(E2)[:, 1], ALU.add))
        link(V.tensor_tensor(OW[:, 0], OW[:, 0], OW[:, 1], ALU.add))
        link(V.tensor_tensor(OS[:], OS[:], VSC[:], ALU.mult))
        V.tensor_tensor(PJ[:, 0:4, SEQ:T], OW[:, 0], OS[:], ALU.add).then_inc(sample_o, 1)

        ve.wait_ge(sample_o, 1)
        ve.wait_ge(go_copied, 16)
        for t in range(KT + 2):
            if t < KT:
                if t >= 2:
                    ve.wait_ge(mix_summed, t - 1)
                V.tensor_scalar(SQ[:, t % 2], PJ[:, t], -SQUARE_OVERFLOWS, SQUARE_OVERFLOWS, ALU.max, ALU.min).then_inc(mix_held, 1)
            if 1 <= t <= KT:
                q = t - 1
                ve.wait_ge(mix_root, q + 1)
                link(V.reciprocal(RS[:, q % 2], RS[:, q % 2]))
                link(V.tensor_scalar(pair(UF[:, 0]), PS[:, 4 + 2 * (q % 2):6 + 2 * (q % 2), 0:HALF], SQUARE_OVERFLOWS ** 2 / 256, 1.0 / 32,
                                     ALU.is_lt, ALU.mult))
                link(V.tensor_tensor(RS[:, q % 2], RS[:, q % 2], UF[:, 0], ALU.mult))
                gain = GD8[:] if q < 4 else VEC2[:, 3:4]
                if q >= 2:
                    ve.wait_ge(hf_ready, 8 + q)
                    ve.wait_ge(h_ready, 8 + q - 1)
                if q < 4:
                    V.scalar_tensor_tensor(TMP[:, q % 2], PJ[:, q], gain, RS[:, q % 2], ALU.mult, ALU.mult).then_inc(hf_ready, 1)
                else:
                    link(V.scalar_tensor_tensor(UF[:, 1], PJ[:, q], gain, RS[:, q % 2], ALU.mult, ALU.mult))
                    ve.wait_ge(silu_ready, q - 3)
                    V.tensor_tensor(TMP[:, q % 2], UF[:, 1], PJ[:, 16 + q], ALU.mult).then_inc(hf_ready, 1)
            if t >= 2:
                set_lo(1, t - 2)
        split_lo(Chunk(C_OUT0))

        def copies(c0, dst):
            for j in range(4 if dst is ACC else 8):
                ch = Chunk(c0 + j)
                split_lo(Chunk(c0 + j + 1))
                for i in range(2):
                    if ch.par[i] == 1:
                        ve.wait_ge(tiles_done, ch.done[i])
                        V.tensor_copy(pair(dst[:, 2 * j + i]), banks(1)).then_inc(banks_free[1], 1)

        def mlp(layer, c0):
            link(V.memset(ACC[:], 0.0))
            with ve.Fori(0, 4) as g:
                for j in range(8):
                    split_lo(Chunk(c0 + j + 1, g))
                    ch = Chunk(c0 + j, g)
                    if j < 4:
                        for i in range(2):
                            u = 32 * layer + 2 * j + i
                            ve.wait_ge(uf_ready, g * 8 + (u + 1))
                            V.tensor_copy(U_hi[:, 2 * j + i], UF[:, i]).then_inc(u_hi_ready, 1)
                            ve.wait_ge(u_hi_ready, g * 8 + (u + 1))
                            V.tensor_tensor(U_lo[:, 2 * j + i], UF[:, i], U_hi[:, 2 * j + i].bitcast(F32), ALU.subtract).then_inc(u_lo_ready, 1)
                    else:
                        for i in range(2):
                            m = 2 * (j - 4) + i
                            ve.wait_ge(tiles_done, ch.done[i])
                            V.tensor_tensor(pair(ACC[:, m]), pair(ACC[:, m]), banks(ch.par[i]), ALU.add).then_inc(banks_free[ch.par[i]], 1)

        copies(C_OUT0, ACC)
        post(1, 0, 8)
        normed(2, 2, 16)
        mlp(0, C_MLP0)
        post(3, 1, 24)
        normed(4, 3, 32)
        copies(C_IN1, GX)

        for kt in range(KT):
            xb = GX[:, KT + kt]
            w = lambda j: VEC[:, V_CONVW + 8 * j + kt:V_CONVW + 8 * j + kt + 1]
            mt = first_tile(C_IN1) + KT + kt
            ve.wait_ge(banks_free[mt % 2], mt // 2 + 1)
            if kt >= 2:
                ve.wait_ge(gates_done, kt - 1)
            if kt >= 2:
                ve.wait_ge(ix_ready, kt - 1)
            xc = XC[:, kt % 2]
            link(V.tensor_scalar(xc, xb, w(3), VEC[:, V_CONVB + kt:V_CONVB + kt + 1], ALU.mult, ALU.add))
            for j in (2, 1, 0):
                back = CONV_W - 1 - j
                V.scalar_tensor_tensor(xc[:, back:SEQ], xb[:, 0:SEQ - back], w(j), xc[:, back:SEQ], ALU.mult, ALU.add)
                t = V.scalar_tensor_tensor(xc[:, SEQ:T], STATE[:, kt, j:24:3], w(j), xc[:, SEQ:T], ALU.mult, ALU.add)
                if j:
                    link(t)
            t.then_inc(xc_ready, 1)
            if kt >= 1:
                input_gate(ve, kt - 1)
        input_gate(ve, KT - 1)
        ve.wait_ge(sp_ln, 1)
        link(V.tensor_scalar(SPT[:, 1], VEC[:, V_LAM:V_LAM + KT], -1.0, 0.0, ALU.mult, ALU.max))
        link(V.tensor_tensor(SPT[:, 1], SPT[:, 1], SPT[:, 0], ALU.add))
        V.tensor_scalar(SPC[:], SPT[:, 1], -RG_C, None, ALU.mult).then_inc(spc_ready, 1)
        for kt in range(KT):
            ve.wait_ge(th_ready, kt + 1)
            if kt >= 2:
                ve.wait_ge(em_ready, kt - 1)
            link(V.tensor_scalar(SQ[:, kt % 2], RG[:, kt], -1.0, 1.0, ALU.mult, ALU.add))
            link(V.reciprocal(SQ[:, kt % 2], SQ[:, kt % 2]))
            V.scalar_tensor_tensor(RG[:, kt], RG[:, kt], -2.0, SQ[:, kt % 2], ALU.mult, ALU.mult).then_inc(em_ready, 1)
        for kt in range(KT):
            ve.wait_ge(sqrt_ready, kt + 1)
            link(V.tensor_tensor(INP[:, kt], INP[:, kt], RG[:, kt], ALU.mult))
            V.tensor_tensor_scan(RG[:, kt, 0:SEQ], DEC[:, kt, 0:SEQ], INP[:, kt, 0:SEQ], 0.0, ALU.mult, ALU.add)
            link(V.tensor_tensor(RG[:, kt, SEQ:T], DEC[:, kt, SEQ:T], STATE[:, kt, 24:32], ALU.mult))
            link(V.tensor_tensor(RG[:, kt, SEQ:T], RG[:, kt, SEQ:T], INP[:, kt, SEQ:T], ALU.add))
            V.tensor_copy(HL[:, kt], RG[:, kt, SEQ - 1:T]).then_inc(hl_ready, 1)
            ve.wait_ge(gelu_ready, kt + 1)
            ve.wait_ge(hl_ready, kt + 1)
            if kt >= 2:
                ve.wait_ge(h_ready, 32 + kt - 1)
            V.tensor_tensor(TMP[:, kt % 2], GX[:, kt], RG[:, kt], ALU.mult).then_inc(hf_ready, 1)
            if kt >= 1:
                set_lo(4, kt - 1)
        set_lo(4, KT - 1)

        copies(C_OUT1, ACC)
        post(5, 2, 40)
        normed(6, 5, 48)
        mlp(1, C_MLP1)
        post(7, 3, 56)

    @block.tensor
    def _(pe):
        MM_ = nc.tensor.matmul
        TR = nc.tensor.transpose

        pe.wait_ge(const_loaded, 16)
        pe.wait_ge(x_loaded, 16 * 5)
        for kt in range(KT):
            if kt >= 4:
                pe.wait_ge((xt_copied_even, xt_copied_odd)[kt % 2], (kt - 4) // 2 + 1)
            for tb in range(4):
                t = TR(PS[:, kt % 4, P * tb:P * tb + P], XIN[:, tb, P * kt:P * kt + P], IDENT)
            t.then_inc(xt_done, 1)
        pe.wait_ge(rows_loaded, 16 * 11)
        for kt in range(KT):
            TR(PS[:, 4, 8 * kt:8 * kt + 8], XSIN[:, P * kt:P * kt + P], IDENT[0:8, 0:8])
            TR(PS[:, 6, 32 * kt:32 * kt + 32], SROWS[:, P * kt:P * kt + P], IDENT[0:32, 0:32])
        TR(PS[:, 5, 0:P], VROWS[:], IDENT)
        TR(PS[:, 5, P:P + 4], VROWS2[:], IDENT[0:4, 0:4]).then_inc(xt_done, 1)
        pe.wait_ge(ones_set, 1)
        pe.wait_ge(tab_loaded, 32)
        pe.wait_ge(vec_ready, 1)
        MM_(PS[0:4, 7, :], TAB[:], HOT[:, 0:512], start=True, stop=True)
        MM_(PS[0:4, 6, 256:384], TAB[:], HOT[:, 512:GREV], start=True, stop=True).then_inc(g_done, 1)

        def sum_squares(n):
            if n >= 1:
                pe.wait_ge(root_ready, n)
            for kt in range(KT):
                pe.wait_ge(sq_ready, 8 * n + kt + 1)
                for i, half in enumerate(halves):
                    t = MM_(PS[:, 4 + i, 0:HALF], ONES[:], SQ[:, kt % 2, half], start=kt == 0, stop=kt == KT - 1)
                t.then_inc(sq_summed, 1)

        def products(ch, hi, lo, ready=None):
            pe.wait_ge(w_lo_ready, ch.ready)
            for i in range(ch.count):
                if ch.tiles[i] >= 2:
                    pe.wait_ge(banks_free[ch.par[i]], ch.banks_free[i])
                cols = slice(P * i, P * i + P)
                for k in range(KT):
                    if ready and i == 0:
                        ready(k)
                    for n, (w, x) in enumerate(((W_hi, hi), (W_hi, lo), (W_lo, hi))):
                        for j, half in enumerate(halves):
                            t = MM_(PS[:, 2 * ch.par[i] + j, 0:HALF], w[:, ch.slot, k, cols], x[:, k, half],
                                    start=k == 0 and n == 0, stop=k == KT - 1 and n == 2)
                t.then_inc(tiles_done, 1)

        def set_ready(m):
            return lambda k: pe.wait_ge(h_ready, 8 * m + k + 1)

        def stage(c0, count, m):
            for j in range(count):
                products(Chunk(c0 + j), H_hi, H_lo, set_ready(m) if j == 0 else None)

        def mlp(layer, c0, m):
            pe.wait_ge(h_ready, 8 * m + 8)
            with pe.Fori(0, 4) as g:
                for j in range(4):
                    products(Chunk(c0 + j, g), H_hi, H_lo)
                for j in range(4, 8):
                    products(Chunk(c0 + j, g), U_hi, U_lo,
                             (lambda k: pe.wait_ge(u_lo_ready, g * 8 + (32 * layer + k + 1))) if j == 4 else None)

        sum_squares(0)
        for c in range(IN_CHUNKS):
            products(Chunk(c), H_hi, H_lo, set_ready(0) if c == 0 else None)
            if c == 2:
                pe.wait_ge(banks_free[0], 2)
                pe.wait_ge(banks_free[1], 2)
                pe.wait_ge(scratch_written, 16)
                for h in range(HEADS):
                    t = TR(PS[0:8, 6, P * h:P * h + P], PJ[:, h, SEQ:T], IDENT)
                t.then_inc(q_rows_done, 1)
            if c == 3:
                pe.wait_ge(q_rows_copied, 1)
                for g in range(2):
                    MM_(PS[:, 6 + g, :], CONST[0:8, C_SEL + P * g:C_SEL + P * g + P], QTOK[:], start=True, stop=True).then_inc(qb_done, 1)

        pe.wait_ge(banks_free[0], 13)
        pe.wait_ge(banks_free[1], 12)
        for i in range(12):
            tb, what = divmod(i, 3)
            if i >= 4:
                pe.wait_ge(tr_copied, i - 3)
            for h in range(HEADS):
                t = TR(PS[:, i % 4, P * h:P * h + P], PJ[:, (4, 8, 16)[what] + h, P * tb:P * tb + P], IDENT)
            t.then_inc(tr_done, 1)
        pe.wait_ge(tr_copied, 12)
        for i, off in enumerate((4, 8, 16)):
            for h in range(HEADS):
                t = TR(PS[0:8, i, P * h:P * h + P], PJ[:, off + h, SEQ:T], IDENT)
            t.then_inc(tr_done, 1)
        pe.wait_ge(bias_loaded, 32)
        pe.wait_ge(qb_copied, 2)
        for h in range(HEADS):
            MM_(PS[:, 4 + h, :], EXCHANGE[:], FLIPPED[:, h], start=True, stop=True).then_inc(flip_done, 1)
        pe.wait_ge(bias_ready, 1)
        pe.wait_ge(wa2_loaded, 16)
        pe.wait_ge(qb_copied, 2)
        for hp in range(2):
            for i, half in enumerate(halves):
                t = MM_(PS[:, 4 + 2 * hp + i, 0:HALF], WA2[:, P * hp:P * hp + P], LR[0:RANK, half], start=True, stop=True)
            t.then_inc(la_done, 1)
        pe.wait_ge(sample_in, 1)
        pe.wait_ge(ln_ready, 1)
        for c in range(2):
            rows = slice(64 * c, 64 * c + 64)
            t = MM_(PS[:, 4 + c, 0:32], ONES[rows], QKP[rows].rearrange("p h b -> p (h b)"), start=True, stop=True)
        t.then_inc(nt_done, 1)
        pe.wait_ge(kd_ready, 2)
        pe.wait_ge(tr_copied, 15)
        for par in range(2):
            rows = slice(64 * par, 64 * par + 64)
            MM_(PS[:, par, 0:16], ONES[rows], AKS[rows].rearrange("p h b -> p (h b)"), start=True, stop=True)
        pe.wait_ge(s0_loaded, 32)
        for par in range(2):
            rows = slice(64 * par, 64 * par + 64)
            for hp in range(2):
                for b in range(N_SAMPLE):
                    t = MM_(PS[:, 2 + par, 8 * hp + b:8 * hp + b + 1], S0[rows, b, hp], QES[rows, hp, b:b + 1], start=True, stop=True)
        t.then_inc(gs_done, 1)
        pe.wait_ge(rsel_ready, 1)
        pe.wait_ge(sn_ready, 2)
        for b in range(N_SAMPLE):
            if b >= 2:
                pe.wait_ge(gs_v_used, b - 1)
            MM_(PS[:, 4 + b % 2, :], RSEL[:, b], GVTOK[:], start=True, stop=True).then_inc(gs_v_done, 1)

        def scores(u):
            h, qb = UNITS[u]
            if u:
                pe.wait_ge(sc_used, u)
            for c in range(2):
                rows = slice(64 * c, 64 * c + 64)
                t = MM_(PS[:, c, 0:P * (qb + 1)], PJ[rows, h, P * qb:P * qb + P], PJ[rows, 4 + h, 0:P * (qb + 1)], start=True, stop=True)
            t.then_inc(sc_done, 1)

        pe.wait_ge(go_s_ready, 2)
        scores(0)
        for u, (h, qb) in enumerate(UNITS):
            if u + 1 < len(UNITS):
                scores(u + 1)
            pe.wait_ge(ad_ready, u + 1)
            if u:
                pe.wait_ge(at_copied, u)
            for kb in range(qb + 1):
                t = TR(PS[:, 2, P * kb:P * kb + P], AD[:, P * kb:P * kb + P], IDENT)
            t.then_inc(at_done, 1)
            pe.wait_ge(at_copied, u + 1)
            if u:
                pe.wait_ge(o_copied, u)
            for kb in range(qb + 1):
                t = MM_(PS[:, 3, 0:P], VT[:, kb, P * h:P * h + P], AT[:, P * kb:P * kb + P], start=kb == 0, stop=kb == qb)
            t.then_inc(o_done, 1)
        pe.wait_ge(o_copied, len(UNITS))

        def softmax(g):
            pe.wait_ge(smx_ready, g + 1)
            TR(PS[0:8, 6, 0:P], ROWMX[:], IDENT).then_inc(smt_done, 1)
            pe.wait_ge(smexp_ready, g + 1)
            TR(PS[:, 6, 128:136], MEXP[:].rearrange("j b n -> j (b n)"), IDENT[0:8, 0:8])
            MM_(PS[:, 6, 256:288], ONES[0:8], MDIAG[:].rearrange("j b i -> j (b i)"), start=True, stop=True).then_inc(smb_done, 1)
            pe.wait_ge(ssum_ready, g + 1)
            MM_(PS[:, 6, 288:320], ONES[:], ZS[:].rearrange("p b j -> p (b j)"), start=True, stop=True).then_inc(smz_done, 1)

        def v_chunks(n0, count):
            for n in range(n0, n0 + count):
                i, g = place("v", n), n // 32
                pe.wait_ge(kv_loaded[i % 4], 16 * (i // 4 + 1))
                pe.wait_ge(pm_ready, n // 4 + 1)
                for pos in range(4):
                    for h in range(HEADS):
                        first = n % 32 == 0 and pos == 0 and h == 0
                        last = n % 32 == 31 and pos == 3 and h == 3
                        t = MM_(PS[:, 7, 32 * g + 8 * h:32 * g + 8 * h + 8], KV[:, i % 4, pos, P * h:P * h + P],
                                PM[:, (n // 4) % 2, 4 * (n % 4) + pos, :, 2 * h:2 * h + 2], start=first, stop=last,
                                skip_group_check=True)
                t.then_inc(v_used, 1)

        softmax(0)
        for u, (tb, hp) in enumerate(GLA_UNITS):
            v_chunks(4 * u, 4)
            block_cols = slice(P * tb, P * tb + P)
            if u:
                pe.wait_ge(kdm_ready, u)
            TR(PS[:, 6, 384:512], KD[:, hp, block_cols], IDENT).then_inc(kdt_done, 1)
            for par in range(2):
                rows = slice(64 * par, 64 * par + 64)
                if u:
                    pe.wait_ge(attm_ready, 2 * (u - 1) + par + 1)
                MM_(PS[:, par, 0:P], KE[rows, hp, block_cols], QE[rows, hp, block_cols], start=True, stop=True).then_inc(att_done, 1)
            pe.wait_ge(kdm_ready, u + 1)
            if u:
                pe.wait_ge(st_ready, 8 * u)
            for n in range(8):
                for par in range(2):
                    h, rows = 2 * hp + par, slice(64 * par, 64 * par + 64)
                    t = MM_(PS[rows, 4 + n // 4, P * (n % 4):P * (n % 4) + P], KDM[:, n, 64 * par:64 * par + 64],
                            GVT[:, tb, P * h:P * h + P], start=True, stop=True)
            t.then_inc(u_done, 1)
            for par in range(2):
                h, rows = 2 * hp + par, slice(64 * par, 64 * par + 64)
                pe.wait_ge(attm_ready, 2 * u + par + 1)
                if u:
                    pe.wait_ge(go_copied, 2 * (u - 1) + par + 1)
                MM_(PS[:, 2 + par, 0:P], GVT[:, tb, P * h:P * h + P], ATTM[:, par], start=True, stop=False)
                for n in range(8):
                    if n:
                        pe.wait_ge(st_ready, 8 * u + n)
                    else:
                        pe.wait_ge(st_first, max(2, u + 1))
                    t = MM_(PS[:, 2 + par, GLA_CHUNK * n:GLA_CHUNK * n + GLA_CHUNK], ST[rows, hp, n],
                            QE[rows, hp, P * tb + GLA_CHUNK * n:P * tb + GLA_CHUNK * (n + 1)], start=False, stop=n == 7)
                t.then_inc(go_done, 1)
        softmax(1)
        v_chunks(32, 32)

        for t_ in range(KT):
            pe.wait_ge(mix_sq, t_ + 1)
            if t_ >= 2:
                pe.wait_ge(hf_ready, 8 + t_ - 1)
            for i, half in enumerate(halves):
                t = MM_(PS[:, 4 + 2 * (t_ % 2) + i, 0:HALF], ONES[:], SQ[:, t_ % 2, half], start=True, stop=True)
            t.then_inc(mix_summed, 1)

        stage(C_OUT0, 4, 1)
        sum_squares(1)
        sum_squares(2)
        mlp(0, C_MLP0, 2)
        sum_squares(3)
        sum_squares(4)
        stage(C_IN1, 8, 3)
        pe.wait_ge(banks_free[0], first_tile(C_OUT1) // 2 + first_tile(C_OUT1) % 2)
        pe.wait_ge(banks_free[1], first_tile(C_OUT1) // 2)
        for kt in range(KT):
            t = TR(PS[0:11, 6 + kt // 4, P * (kt % 4):P * (kt % 4) + P], GX[:, KT + kt, SEQ - 3:T], IDENT)
        t.then_inc(xrows_done, 1)
        pe.wait_ge(gates_loaded, 32)
        for kt in range(KT):
            pe.wait_ge(xc_ready, kt + 1)
            if kt:
                pe.wait_ge(r_ready, kt)
                pe.wait_ge(i_ready, kt)
            for w in range(2):
                for i, half in enumerate(halves):
                    t = MM_(PS[:, 2 * w + i, 0:HALF], WG[w][:, kt], XC[:, kt % 2, half], start=True, stop=True)
            t.then_inc(gates_done, 1)
        pe.wait_ge(hl_ready, KT)
        for kt in range(KT):
            t = TR(PS[0:9, 4 + kt // 4, P * (kt % 4):P * (kt % 4) + P], HL[:, kt], IDENT)
        t.then_inc(hrows_done, 1)
        pe.wait_ge(i_ready, KT)
        stage(C_OUT1, 4, 4)
        pe.wait_ge(hrows_copied, 1)
        sum_squares(5)
        sum_squares(6)
        mlp(1, C_MLP1, 5)
        sum_squares(7)
        pe.wait_ge(x_even, 16)
        pe.wait_ge(x_odd, 16)
        for tb in range(4):
            if tb >= 2:
                pe.wait_ge(yt_copied, tb - 1)
            for kt in range(KT):
                t = TR(PS[:, 2 * (tb % 2) + kt // 4, P * (kt % 4):P * (kt % 4) + P], X[:, kt, P * tb:P * tb + P], IDENT)
            t.then_inc(yt_done, 1)
        pe.wait_ge(root_ready, 8)
        for kt in range(KT):
            t = TR(PS[0:8, 4 + kt // 4, P * (kt % 4):P * (kt % 4) + P], X[:, kt, SEQ:T], IDENT)
        t.then_inc(yt_done, 1)


_OUTS = [("y_prompt", (1, SEQ, D_MODEL)), ("y_sample", (N_SAMPLE, 1, D_MODEL)),
         ("k_prompt", (1, 1, SEQ, HEADS, P)), ("v_prompt", (1, 1, SEQ, HEADS, P)),
         ("k_sample", (1, N_SAMPLE, 1, HEADS, P)), ("v_sample", (1, N_SAMPLE, 1, HEADS, P)),
         ("gla_prompt", (1, 1, HEADS, DH, P)), ("gla_sample", (1, N_SAMPLE, HEADS, DH, P)),
         ("conv_prompt", (1, 1, CONV_W - 1, D_MODEL)), ("conv_sample", (1, N_SAMPLE, CONV_W - 1, D_MODEL)),
         ("rglru_prompt", (1, 1, D_MODEL)), ("rglru_sample", (1, N_SAMPLE, D_MODEL))]


def build(nc, a, o):
    views = {
        "y_prompt": o["y_prompt"][0], "y_sample": o["y_sample"].rearrange("b t d -> (b t) d"),
        "k_prompt": o["k_prompt"][0, 0].rearrange("t h d -> t (h d)"), "v_prompt": o["v_prompt"][0, 0].rearrange("t h d -> t (h d)"),
        "k_sample": o["k_sample"][0].rearrange("b t h d -> (b t) (h d)"), "v_sample": o["v_sample"][0].rearrange("b t h d -> (b t) (h d)"),
        "gla_prompt": o["gla_prompt"][0, 0].rearrange("(hp q) k v -> hp (q k) v", q=2), "gla_sample": o["gla_sample"][0],
        "conv_prompt": o["conv_prompt"][0, 0], "conv_sample": o["conv_sample"][0],
        "rglru_prompt": o["rglru_prompt"][0], "rglru_sample": o["rglru_sample"][0]}
    with ExitStack() as ctx:
        trunk(nc, ctx, a, views)


def kernel(**inputs):
    import numpy as _np
    import concourse.bacc as _bacc
    from concourse import mybir as _mybir
    from concourse.bass_utils import run_bass_kernel_spmd as _run

    nc = _bacc.Bacc("TRN2", target_bir_lowering=False, num_devices=1)
    arrays, args, outs = {}, {}, {}
    for name, x in [*inputs.items(), ("consts", constant_table())]:
        x = _np.ascontiguousarray(x)
        arrays[f"in_{name}"] = x
        args[name] = nc.dram_tensor(f"in_{name}", x.shape, _mybir.dt.from_np(x.dtype), kind="ExternalInput").ap()
    for name, shape in _OUTS:
        outs[name] = nc.dram_tensor(f"out_{name}", shape, _mybir.dt.float32, kind="ExternalOutput").ap()
    build(nc, args, outs)
    r = _run(nc, [arrays], core_ids=[0])
    return tuple(r.results[0][f"out_{name}"] for name, _ in _OUTS)
```

```python
import math
from contextlib import ExitStack

import numpy as np
import concourse.bass as bass
from concourse import mybir

F32 = mybir.dt.float32
F32R = mybir.dt.float32r
I32 = mybir.dt.int32
ALU = mybir.AluOpType
ACT = mybir.ActivationFunctionType
AX = mybir.AxisListType

P = 128
D_MODEL = 1024
SEQ = 512
N_SAMPLE = 8
T = SEQ + N_SAMPLE
HALF = T // 2
KT = D_MODEL // P
N_POOL, PAGE, N_PAGES = 320, 128, 32
HEADS, DH = 4, 64
SCALE = DH ** -0.5
GLA_CHUNK, GLA_TAU, RANK = 16, 16.0, 16
D_IN = 3088
D_FF = 4096
BUCKETS, MAX_DISTANCE = 32, 128
EPS = 1e-6
NEG = -1e30
LAM_INIT = 0.8 - 0.6 * math.exp(0.0)
RG_C = 8.0
CONV_W = 4
SQUARE_OVERFLOWS = 2.0 ** 64

GREV = 640
C_IDENT, C_ATT, C_CHUNK, C_GROUP, C_SEL, C_HOT = 0, 128, 256, 264, 268, 268 + 256
C_EXCH = C_HOT + GREV
C_COLS = C_EXCH + P


def constant_table():
    c = np.zeros((P, C_COLS), np.float32)
    p = np.arange(P)
    c[:, C_IDENT:C_IDENT + P] = np.eye(P)
    s, t = p[:, None], p[None, :]
    c[:, C_ATT:C_ATT + P] = (s <= t) & (s // GLA_CHUNK == t // GLA_CHUNK)
    c[p, C_EXCH + 127 - p] = 1
    c[p, C_CHUNK + p // GLA_CHUNK] = 1
    c[p, C_GROUP + p // N_PAGES] = 1
    for g in range(2):
        c[4 * g + p // N_PAGES, C_SEL + P * g + p] = 1
    rel = 511 - np.arange(GREV)
    exact = BUCKETS // 2
    far = exact + (np.log(np.maximum(rel, 1).astype(np.float32) / exact)
                   / math.log(MAX_DISTANCE / exact) * (BUCKETS - exact)).astype(np.int32)
    bucket = np.where(rel < exact, rel, np.minimum(far, BUCKETS - 1))
    bucket = np.where(rel < 0, BUCKETS, bucket)
    c[bucket, C_HOT + np.arange(GREV)] = 1
    return c


IN_CHUNKS = 13
C_OUT0 = IN_CHUNKS
C_MLP0 = C_OUT0 + 4
C_IN1 = C_MLP0 + 32
C_OUT1 = C_IN1 + 8
C_MLP1 = C_OUT1 + 4
N_CHUNKS = C_MLP1 + 32


def first_tile(c):
    return 2 * c if c < IN_CHUNKS else 2 * c - 1


class Chunk:

    def __init__(self, c, g=None):
        self.static = c
        self.slot = c % 2
        self.count = 1 if c == IN_CHUNKS - 1 else 2
        at = lambda value, per_group: value if g is None else g * per_group + value
        self.ready = at(c + 1, 8)
        self.loaded = at(16 * (c // 2 + 1), 64)
        self.slot_free = at(c - 1, 8)
        self.prev_done = at(first_tile(c - 1) if c >= 2 else 0, 16)
        self.tiles = [first_tile(c) + i for i in range(self.count)]
        self.par = [m % 2 for m in self.tiles]
        self.done = [at(m + 1, 16) for m in self.tiles]
        self.banks_free = [at(m // 2, 8) for m in self.tiles]


def trunk(nc, ctx, a, o):
    x_in = a["x_prompt"][0]
    xs_in = a["x_sample"].rearrange("b t d -> (b t) d")
    cache = {"k": a["cache_k"], "v": a["cache_v"]}
    cache = {n: c.rearrange("l n (c q) h d -> (l n c) (q h d)", q=4) for n, c in cache.items()}

    base = -(-nc.sbuf_base // 64) * 64
    top = [base]

    def region(size):
        at = top[0]
        top[0] += -(-size // 32) * 32
        assert top[0] <= nc.sbuf_usable_end, top[0]
        return at

    def sb(name, shape, dt, at):
        return nc.alloc_sbuf_tensor_at(name, shape, dt, offset=at)

    TB = 4 * T
    X = sb("X", [P, KT, T], F32, region(KT * TB))
    r_h = region(2 * KT * TB)
    r_raw = region(2 * 8192)
    r_w = region(4 * 8192)
    r_1 = region(3 * KT * TB)
    r_kv = region(2 * KT * TB)
    r_t = region(20736)
    r_c = region(0)

    H_hi = sb("H_hi", [P, KT, T], F32R, r_h)
    H_lo = sb("H_lo", [P, KT, T], F32R, r_h + KT * TB)
    RAW = sb("RAW", [P, 2, KT, 256], F32, r_raw)
    W_hi = sb("W_hi", [P, 2, KT, 256], F32R, r_w)
    W_lo = sb("W_lo", [P, 2, KT, 256], F32R, r_w + 16384)

    XIN = sb("XIN", [P, 4, D_MODEL], F32, r_1)
    XSIN = sb("XSIN", [N_SAMPLE, D_MODEL], F32, r_1 + 16384)
    VROWS = sb("VROWS", [P, P], F32, r_1 + 20480)
    VROWS2 = sb("VROWS2", [4, P], F32, r_1 + 20992)
    SROWS = sb("SROWS", [32, D_MODEL], F32, r_1 + 21504)
    LAMIN = sb("LAMIN", [P, 4, DH], F32, r_1 + 25600)
    LAMPR = sb("LAMPR", [P, 2, DH], F32, r_1 + 26624)
    HOT = sb("HOT", [33, GREV], F32, r_1 + 27648)
    GSB = sb("GSB", [4, GREV], F32, r_1 + 30720)
    PJ = sb("PJ", [P, 24, T], F32, r_1)
    U_hi = sb("U_hi", [P, KT, T], F32R, r_1)
    U_lo = sb("U_lo", [P, KT, T], F32R, r_1 + KT * TB)
    ACC = sb("ACC", [P, KT, T], F32, r_1 + 2 * KT * TB)
    GX = sb("GX", [P, 2 * KT, T], F32, r_1)
    RG = ACC

    KV = sb("KV", [P, 4, 4, 512], F32, r_kv)
    DEC = sb("DEC", [P, KT, T], F32, r_kv)
    INP = sb("INP", [P, KT, T], F32, r_kv + KT * TB)
    PROD = sb("PROD", [P, 2, 2, 512], F32, r_t)
    SC = [sb(f"SC{g}", [P, 8, PAGE], F32, r_t + 8192 + 4096 * g) for g in range(2)]
    LR = sb("LR", [P, T], F32, r_t + 12288)
    QB = sb("QB", [P, 2, 512], F32, r_t + 16384)
    SQ = sb("SQ", [P, 2, T], F32, r_t)
    TMP = sb("TMP", [P, 2, T], F32, r_t + 2 * TB)
    RS = sb("RS", [P, 2, T], F32, r_t + 4 * TB)
    UF = sb("UF", [P, 2, T], F32, r_t + 6 * TB)
    RL = SQ
    XC = UF
    YT = sb("YT", [P, 2, D_MODEL], F32, r_kv)
    YS = sb("YS", [N_SAMPLE, D_MODEL], F32, r_kv + 8192)
    WG = [sb(f"WG{i}", [P, KT, P], F32, r_w + 4096 * i) for i in range(2)]

    VT = sb("VT", [P, 4, 512], F32, r_w)
    GVT = sb("GVT", [P, 4, 512], F32, r_w + 8192)
    PR = sb("PR", [P, 2, 512], F32, r_w + 16384)
    AD = sb("AD", [P, 512], F32, r_w + 20480)
    AT = sb("AT", [P, 512], F32, r_w + 22528)
    BC = sb("BC", [P, 2, SEQ], F32, r_w + 24576)
    KDM = sb("KDM", [P, 8, P], F32, r_w + 28672)
    KSTAGE = PR
    HSQ = sb("HSQ", [P, 2, SEQ], F32, r_w)
    HTMP = sb("HTMP", [P, 2, SEQ], F32, r_w + 4096)
    HRS = sb("HRS", [P, 2, SEQ], F32, r_w + 16384)
    HUF = sb("HUF", [P, 2, SEQ], F32, r_w + 20480)
    XL = sb("XL", [P, 3, T], F32, r_w + 16384)
    BIAS = sb("BIAS", [P, HEADS, 512], F32, r_h)
    SBIAS = sb("SBIAS", [P, HEADS, PAGE], F32, r_h + 8192)
    FLIPPED = sb("FLIPPED", [P, HEADS, 512], F32, r_h + 10240)
    EXCHANGE = sb("EXCHANGE", [P, P], F32, r_h + 31744)
    QE = sb("QE", [P, 2, SEQ], F32, r_h + 10240)
    KE = sb("KE", [P, 2, SEQ], F32, r_h + 14336)
    KD = sb("KD", [P, 2, SEQ], F32, r_h + 18432)
    ST = sb("ST", [P, 2, 9, P], F32, r_h + 22528)
    ATTM = sb("ATTM", [P, 2, P], F32, r_h + 31744)

    def small(name, cols, dt=F32, rows=P):
        cols = list(cols) if isinstance(cols, (list, tuple)) else [cols]
        return sb(name, [rows, *cols], dt, region(4 * int(np.prod(cols))))

    CONST = small("CONST", C_HOT)
    IDENT = CONST[:, C_IDENT:C_IDENT + P]
    ATTMASK = CONST[:, C_ATT:C_ATT + P].bitcast(I32)
    CHUNKMASK = CONST[:, C_CHUNK:C_CHUNK + 8]
    GROUPMASK = CONST[:, C_GROUP:C_GROUP + 4]
    ONES = small("ONES", P)
    VEC = small("VEC", P)
    VEC2 = small("VEC2", 4)
    STATE = small("STATE", [KT, 32])
    V_CONVW, V_CONVB, V_BA, V_BX, V_LAM = 64, 96, 104, 112, 120
    EPSC = small("EPSC", 2)
    PIDX = small("PIDX", 2, I32)
    CIDX = [small(f"CIDX{g}", 1, I32) for g in range(2)]
    WA2 = small("WA2", 256, rows=RANK)
    LAM = small("LAM", 4)
    TAB = small("TAB", 4, rows=33)
    TB0 = small("TB0", 4)
    GD8 = small("GD8", 1)
    MX = small("MX", 2)
    NM = small("NM", 2)
    SM = small("SM", 2)
    RR = small("RR", 2)
    ROWMX = small("ROWMX", 8)
    NROW = small("NROW", 8)
    ROWSUM = small("ROWSUM", 8)
    M84 = small("M84", 4, rows=8)
    MEXP = sb("MEXP", [8, 4, 32], F32, r_h + 32768)
    MDIAG = small("MDIAG", [4, 8], rows=8)
    ZS = small("ZS", [4, 8])
    MP = small("MP", [2, 4, 8])
    ZP = small("ZP", [2, 4, 8])
    SN = small("SN", [8, 4, 2])
    MM = small("MM", 64)
    E1 = small("E1", 64)
    E2 = small("E2", 64)
    ZZ = small("ZZ", 64)
    QKP = small("QKP", [HEADS, N_SAMPLE])
    VSC = small("VSC", [HEADS, N_SAMPLE])
    GVC = small("GVC", [HEADS, N_SAMPLE])
    OW = small("OW", [2, HEADS, N_SAMPLE])
    OS = small("OS", [HEADS, N_SAMPLE])
    DECC = small("DECC", [2, 32])
    LAS = small("LAS", [2, 8])
    EAS = small("EAS", [2, 8])
    ENS = small("ENS", [2, 8])
    QES = small("QES", [2, 8])
    KES = small("KES", [2, 8])
    KSS = small("KSS", [2, 8])
    AKS = small("AKS", [2, 8])
    SPC = small("SPC", 8)
    SPT = small("SPT", [2, 8])
    HL = small("HL", [KT, 9])
    S0 = sb("S0", [P, N_SAMPLE, 2, P], F32, r_1 + 8 * TB)
    RSEL = sb("RSEL", [8, 8, P], F32, r_1 + 16 * TB)
    GVTOK = sb("GVTOK", [N_SAMPLE, 512], F32, r_1 + 16 * TB + 4096)
    SCANM = sb("SCANM", [P, SEQ], F32, r_1 + 16 * TB + 6144)
    PM = sb("PM", [P, 2, 16, 4, 8], F32, r_w + 24576)
    KVTOK = sb("KVTOK", [N_SAMPLE, D_MODEL], F32, r_w + 20480)
    QTOK = sb("QTOK", [N_SAMPLE, 512], F32, r_t)
    STOK = sb("STOK", [11, D_MODEL], F32, r_t + 8 * TB)
    WG = [sb(f"WG{i}", [P, KT, P], F32, r_kv + 4096 * i) for i in range(2)]
    HTOK = STOK
    PVT = sb("PVT", [P, HEADS, 2, N_SAMPLE], F32, r_kv + 32768)

    PS = nc.alloc_psum_tensor("PS", [P, 8, 512], F32)

    def sem(name):
        return ctx.enter_context(nc.semaphore(name))

    act_step = sem("act_step")
    ad_ready = sem("ad_ready")
    at_copied = sem("at_copied")
    at_done = sem("at_done")
    att_done = sem("att_done")
    attm_ready = sem("attm_ready")
    bc_ready = sem("bc_ready")
    bias_loaded = sem("bias_loaded")
    bias_ready = sem("bias_ready")
    cidx_ready = sem("cidx_ready")
    const_loaded = sem("const_loaded")
    dve_step = sem("dve_step")
    eb_ready = sem("eb_ready")
    em_ready = sem("em_ready")
    ex_done = sem("ex_done")
    flip_done = sem("flip_done")
    g_done = sem("g_done")
    gates_done = sem("gates_done")
    gates_loaded = sem("gates_loaded")
    pvt_ready = sem("pvt_ready")
    ogt_done = sem("ogt_done")
    og_copied = sem("og_copied")
    go_copied = sem("go_copied")
    go_done = sem("go_done")
    go_s_ready = sem("go_s_ready")
    gs_done = sem("gs_done")
    gs_v_done = sem("gs_v_done")
    gs_v_used = sem("gs_v_used")
    h_ready = sem("h_ready")
    hf_ready = sem("hf_ready")
    hhi_ready = sem("hhi_ready")
    hl_ready = sem("hl_ready")
    hrows_copied = sem("hrows_copied")
    hrows_done = sem("hrows_done")
    i_ready = sem("i_ready")
    idx_loaded = sem("idx_loaded")
    inverse_ready = sem("inverse_ready")
    ix_ready = sem("ix_ready")
    k_used = sem("k_used")
    kd_ready = sem("kd_ready")
    kdm_ready = sem("kdm_ready")
    kdt_done = sem("kdt_done")
    kdx_exp = sem("kdx_exp")
    kdx_ready = sem("kdx_ready")
    la_done = sem("la_done")
    lam_exp = sem("lam_exp")
    lam_loaded = sem("lam_loaded")
    lam_sums = sem("lam_sums")
    ln_ready = sem("ln_ready")
    mix_held = sem("mix_held")
    mix_root = sem("mix_root")
    mix_sq = sem("mix_sq")
    mix_summed = sem("mix_summed")
    new_held = sem("new_held")
    new_sq = sem("new_sq")
    new_summed = sem("new_summed")
    new_root = sem("new_root")
    new_scaled = sem("new_scaled")
    new_hi = sem("new_hi")
    new_ready = sem("new_ready")
    mm_exp = sem("mm_exp")
    mm_ready = sem("mm_ready")
    nm_ready = sem("nm_ready")
    nt_done = sem("nt_done")
    o_copied = sem("o_copied")
    o_done = sem("o_done")
    ones_set = sem("ones_set")
    outputs_written = sem("outputs_written")
    pm_ready = sem("pm_ready")
    post_even = sem("post_even")
    post_odd = sem("post_odd")
    prod1_ready = sem("prod1_ready")
    prod1_used = sem("prod1_used")
    q_rows_copied = sem("q_rows_copied")
    q_rows_done = sem("q_rows_done")
    qb_copied = sem("qb_copied")
    qb_done = sem("qb_done")
    r_ready = sem("r_ready")
    root_ready = sem("root_ready")
    rows_loaded = sem("rows_loaded")
    rsel_ready = sem("rsel_ready")
    s0_loaded = sem("s0_loaded")
    sample_in = sem("sample_in")
    sample_o = sem("sample_o")
    sbias_loaded = sem("sbias_loaded")
    sc_done = sem("sc_done")
    sc_used = sem("sc_used")
    scratch_written = sem("scratch_written")
    silu_ready = sem("silu_ready")
    smb_done = sem("smb_done")
    smexp_ready = sem("smexp_ready")
    smt_done = sem("smt_done")
    smx_ready = sem("smx_ready")
    smz_done = sem("smz_done")
    smzp_done = sem("smzp_done")
    sn_ready = sem("sn_ready")
    snm_ready = sem("snm_ready")
    soft_done = sem("soft_done")
    sp_ln = sem("sp_ln")
    spc_ready = sem("spc_ready")
    sq_ready = sem("sq_ready")
    sq_summed = sem("sq_summed")
    sqrt_ready = sem("sqrt_ready")
    ssum_ready = sem("ssum_ready")
    st_first = sem("st_first")
    st_ready = sem("st_ready")
    tab_loaded = sem("tab_loaded")
    tb0_loaded = sem("tb0_loaded")
    th_ready = sem("th_ready")
    tiles_done = sem("tiles_done")
    tr_copied = sem("tr_copied")
    tr_done = sem("tr_done")
    u_done = sem("u_done")
    u_hi_ready = sem("u_hi_ready")
    u_lo_ready = sem("u_lo_ready")
    uf_ready = sem("uf_ready")
    v_used = sem("v_used")
    vec_ready = sem("vec_ready")
    w_hi_ready = sem("w_hi_ready")
    w_lo_ready = sem("w_lo_ready")
    wa2_loaded = sem("wa2_loaded")
    x_even = sem("x_even")
    x_loaded = sem("x_loaded")
    x_odd = sem("x_odd")
    xc_ready = sem("xc_ready")
    xrows_done = sem("xrows_done")
    xt_copied_even = sem("xt_copied_even")
    xt_copied_odd = sem("xt_copied_odd")
    xt_done = sem("xt_done")
    yt_copied = sem("yt_copied")
    yt_done = sem("yt_done")
    raw_loaded = [sem(f"raw_loaded{i}") for i in range(2)]
    banks_free = [sem(f"banks_free{i}") for i in range(2)]
    kv_loaded = [sem(f"kv_loaded{i}") for i in range(4)]
    k_sent = [sem(f"k_sent{i}") for i in range(2)]
    y_sent = [sem(f"y_sent{i}") for i in range(2)]
    N_OUT = 16
    scratch = nc.dram_tensor("bias_scratch", [HEADS, GREV], F32, kind="Internal").ap()

    def x_first_ready(eng, kt):
        if kt == 0 or eng is nc.vector:
            eng.wait_ge(vec_ready, 1)
            eng.wait_ge(xt_copied_even, 4)
            eng.wait_ge(xt_copied_odd, 4)

    def x_ready(i):
        def ready(eng, kt):
            eng.wait_ge(x_odd if kt % 2 else x_even, 4 * i + kt // 2 + 1)
        return ready

    def input_gate(ve, kt):
        ve.wait_ge(i_ready, kt + 1)
        nc.vector.tensor_tensor(INP[:, kt], TMP[:, kt % 2], XC[:, kt % 2], ALU.mult).then_inc(ix_ready, 1)

    def stage_dram(w, row, col):
        return w.rearrange("(r p) n -> p r n", p=P)[:, row // P:row // P + KT, col]

    def uses(i):
        if i < 32:
            return "k", 0, i
        if i < 96:
            return ("v", 0, (i - 32) // 2) if i % 2 == 0 else ("k", 1, (i - 33) // 2)
        return "v", 1, i - 96

    def place(kind, n):
        if kind == "k":
            return n if n < 32 else 33 + 2 * (n - 32)
        return 32 + 2 * n if n < 32 else 64 + n

    SCALED_BEFORE = {0: 0, 3: 16, 4: 24}
    LOADS = 128
    UNITS = [(h, qb) for h in range(HEADS) for qb in range(4)]
    GLA_UNITS = [(tb, hp) for tb in range(4) for hp in range(2)]
    halves = [slice(0, HALF), slice(HALF, T)]

    def banks(par):
        return PS[:, 2 * par:2 * par + 2, 0:HALF]

    def pair(ap):
        return ap.rearrange("p (s t) -> p s t", s=2)

    ctx.enter_context(nc.allow_non_contiguous_dma(reason="vectors and transposed states"))
    block = ctx.enter_context(nc.Block())

    @block.sync
    def _(sp):
        def load(ch, src):
            if ch.static >= 2:
                sp.wait_ge(w_lo_ready, ch.slot_free)
            sp.dma_start(RAW[:, ch.slot], src).then_inc(raw_loaded[ch.slot], 16)

        w_in = a["w_in_even"][0]
        for c in range(IN_CHUNKS):
            col = 256 * c if c < 10 else 2576 + 256 * (c - 10) if c < 12 else 2560
            load(Chunk(c), stage_dram(w_in, 0, slice(col, col + 256)))
        for j in range(4):
            load(Chunk(C_OUT0 + j), stage_dram(a["w_out_even"][0], 0, slice(256 * j, 256 * j + 256)))

        def mlp(layer, c0):
            up = a["w_up"][layer].rearrange("(r p) n -> p r n", p=P)
            down = a["w_down"][layer].rearrange("(q r p) n -> p q r n", p=P, r=KT)
            with sp.Fori(0, 4) as g:
                for j in range(4):
                    load(Chunk(c0 + j, g), up[:, :, bass.ds(g * 1024 + 256 * j, 256)])
                for j in range(4):
                    load(Chunk(c0 + 4 + j, g), down[:, bass.ds(g, 1), :, 256 * j:256 * j + 256]
                         .rearrange("p q r n -> p (q r) n"))

        mlp(0, C_MLP0)
        for j in range(8):
            load(Chunk(C_IN1 + j), stage_dram(a["w_in_odd"][0], 0, slice(256 * j, 256 * j + 256)))
        for j in range(4):
            load(Chunk(C_OUT1 + j), stage_dram(a["w_out_odd"][0], 0, slice(256 * j, 256 * j + 256)))
        mlp(1, C_MLP1)
        load(Chunk(N_CHUNKS), stage_dram(a["w_out_odd"][0], 0, slice(0, 256)))
        for sent in k_sent:
            sp.wait_ge(sent, 32)
        sp.wait_ge(outputs_written, 16 * N_OUT)

    @block.gpsimd
    def _(po):
        po.wait_ge(cidx_ready, 2)

        def pool_product(n):
            i = place("k", n)
            po.wait_ge(kv_loaded[i % 4], 16 * (i // 4 + 1))
            if n == 0:
                po.wait_ge(qb_copied, 2)
            if n >= 1:
                po.wait_ge(prod1_used, n)
            nc.gpsimd.tensor_tensor(PROD[:, 1], KV[:, i % 4, 2:4, :], QB[:, None, n // 32, :].to_broadcast([P, 2, 512]),
                                    ALU.mult).then_inc(prod1_ready, 1)

        def probabilities(b):
            if b >= 2:
                po.wait_ge(v_used, 4 * (b - 1))
            g, pos = b // 8, 16 * (b % 8)
            if b % 8 == 0:
                po.wait_ge(soft_done, 8 * (g + 1))
            nc.gpsimd.tensor_tensor(
                PM[:, b % 2], SC[g][:, :, pos:pos + 16].rearrange("p j n -> p n j")[:, :, None, :].to_broadcast([P, 16, 4, 8]),
                GROUPMASK[:, None, :, None].to_broadcast([P, 16, 4, 8]), ALU.mult).then_inc(pm_ready, 1)

        def release(i):
            kind, g, cc = uses(i)
            n = 32 * g + cc
            if kind == "k":
                if g == 0:
                    pool_product(n)
                po.wait_ge(k_used, n + 1)
                po.wait_ge(prod1_ready, n + 1)
            else:
                if n % 32 == 0:
                    probabilities(n // 4)
                if n % 4 == 1 and n % 32 < 28:
                    probabilities(n // 4 + 1)
                if g == 0:
                    pool_product(n + 32)
                po.wait_ge(v_used, n + 1)

        for i in range(LOADS + 4):
            if i >= 4:
                if i - 4 < LOADS:
                    release(i - 4)
            if i < LOADS:
                kind, g, cc = uses(i)
                po.indirect_dma_start(KV[:, i % 4].rearrange("p n f -> p (n f)"), None, cache[kind],
                                      bass.IndirectOffsetOnAxis(ap=CIDX[g][:], axis=0),
                                      element_offset=cc * 2048).then_inc(kv_loaded[i % 4], 16)

        def post_add(i):
            for kt in range(1, KT, 2):
                po.wait_ge(post_odd, 4 * i + kt // 2 + 1)
                nc.gpsimd.tensor_tensor(X[:, kt], X[:, kt], TMP[:, 1], ALU.add).then_inc(x_odd, 1)
        for i in range(4):
            post_add(i)

    @block.scalar
    def _(act):
        chain = [0]

        def link(ins):
            chain[0] += 1
            ins.then_inc(act_step, 1)
            act.wait_ge(act_step, chain[0])

        A = nc.scalar.activation

        def out_dma(dst, src):
            act.dma_start(dst, src).then_inc(outputs_written, 16)

        act.dma_start(CONST[:], a["consts"][:, 0:C_HOT]).then_inc(const_loaded, 16)
        for tb in range(4):
            act.dma_start(XIN[:, tb], x_in[P * tb:P * tb + P, :]).then_inc(x_loaded, 16)
        act.dma_start(XSIN[:], xs_in).then_inc(x_loaded, 16)
        act.dma_start(PIDX[:], a["page_table"].rearrange("(g b) n -> g (b n)", g=2).rearrange("g p -> p g")
).then_inc(idx_loaded, 16)
        rows = [(VROWS[0:64], a["norm_g"].rearrange("l i (k p) -> (l i k) p", p=P)),
                (VROWS[64:96], a["conv_w"][0].rearrange("j (k p) -> (j k) p", p=P)),
                (VROWS[96:104], a["conv_b"][0].rearrange("(k p) -> k p", p=P)),
                (VROWS[104:112], a["b_gate_a"][0].rearrange("(k p) -> k p", p=P)),
                (VROWS[112:120], a["b_gate_x"][0].rearrange("(k p) -> k p", p=P)),
                (VROWS[120:128], a["rg_lambda"][0].rearrange("(k p) -> k p", p=P)),
                (VROWS2[0:2], a["b_alpha2"][0].rearrange("(k p) -> k p", p=P)),
                (VROWS2[2:3], a["g_diff"]), (VROWS2[3:4], a["g_gla"]),
                (SROWS[0:24], a["state_conv"][0].rearrange("b j d -> (b j) d")),
                (SROWS[24:32], a["state_rglru"][0])]
        for dst, src in rows:
            act.dma_start(dst, src).then_inc(rows_loaded, 16)
        for i, n in enumerate(("lam_q1", "lam_k1", "lam_q2", "lam_k2")):
            act.dma_start(LAMIN[:, i], a[n].to_broadcast([P, DH])).then_inc(lam_loaded, 16)
        act.dma_start(TAB[0:32], a["rel_table"]).then_inc(tab_loaded, 16)
        act.dma_start(HOT[:], a["consts"][0:33, C_HOT:C_HOT + GREV]).then_inc(tab_loaded, 16)
        act.dma_start(TB0[:], a["rel_table"][0:1, :].to_broadcast([P, 4])).then_inc(tb0_loaded, 16)
        act.dma_start(WA2[:], a["w_alpha2"][0]).then_inc(wa2_loaded, 16)

        for i in range(4):
            act.wait_ge(xt_done, 2 * i + 2)
            A(X[:, 2 * i + 1, 0:SEQ], PS[:, (2 * i + 1) % 4], ACT.Copy).then_inc(xt_copied_odd, 1)
        act.wait_ge(lam_sums, 1)
        A(LAM[:, 0:2], LAM[:, 0:2], ACT.Exp).then_inc(lam_exp, 1)
        act.wait_ge(g_done, 1)
        A(GSB[:, 0:512], PS[0:4, 7, :], ACT.Copy)
        link(A(GSB[:, 512:GREV], PS[0:4, 6, 256:384], ACT.Copy))
        act.dma_start(scratch, GSB[:]).then_inc(scratch_written, 16)

        def split_hi(ch):
            act.wait_ge(raw_loaded[ch.slot], ch.loaded)
            if ch.static >= 2:
                act.wait_ge(tiles_done, ch.prev_done)
            A(W_hi[:, ch.slot], RAW[:, ch.slot], ACT.Copy).then_inc(w_hi_ready, 1)

        def squares(n, src, ready, into=None):
            if into:
                m, gain, before = into
                act.wait_ge(tiles_done, before)
            for kt in range(KT):
                ready(act, kt)
                if into:
                    A(H_hi[:, kt], src[:, kt], ACT.Copy, scale=VEC[:, gain + kt:gain + kt + 1]).then_inc(hhi_ready, 1)
                if 8 * n + kt >= 2:
                    act.wait_ge(sq_summed, 8 * n + kt - 1)
                A(SQ[:, kt % 2], src[:, kt], ACT.Square).then_inc(sq_ready, 1)
            act.wait_ge(sq_summed, 8 * n + 8)
            if n >= 1:
                act.wait_ge(inverse_ready, n)
            A(pair(RS[:, 0]), PS[:, 4:6, 0:HALF], ACT.Sqrt, scale=1.0 / D_MODEL, bias=EPSC[:, 0:1]).then_inc(root_ready, 1)

        def normed_hi(m, before):
            if before:
                act.wait_ge(tiles_done, before)
            for kt in range(KT):
                act.wait_ge(hf_ready, SCALED_BEFORE[m] + kt + 1)
                A(H_hi[:, kt], TMP[:, kt % 2], ACT.Copy).then_inc(hhi_ready, 1)

        squares(0, X, x_first_ready)
        split_hi(Chunk(0))
        normed_hi(0, 0)
        for c in range(IN_CHUNKS):
            if c + 1 < IN_CHUNKS:
                split_hi(Chunk(c + 1))
            ch = Chunk(c)
            for m, par, done in zip(ch.tiles, ch.par, ch.done):
                act.wait_ge(tiles_done, done)
                if m == 12:
                    act.wait_ge(scratch_written, 16)
                if m < 24:
                    A(pair(PJ[:, m]), banks(par), ACT.Copy, scale=SCALE if m < 4 or m in (12, 13) else 1.0).then_inc(banks_free[par], 1)
                else:
                    A(pair(LR[0:RANK]), PS[0:RANK, 0:2, 0:HALF], ACT.Copy).then_inc(banks_free[0], 1)
            if c == 3:
                act.wait_ge(q_rows_done, 1)
                A(QTOK[:], PS[0:8, 6, :], ACT.Copy).then_inc(q_rows_copied, 1)

        act.wait_ge(tiles_done, first_tile(C_OUT0))
        act.wait_ge(scratch_written, 16)
        act.dma_start(FLIPPED[:], bass.AP(scratch.tensor, 0, [[1, P], [GREV, HEADS], [1, 512]])).then_inc(bias_loaded, 16)
        act.dma_start(EXCHANGE[:], a["consts"][:, C_EXCH:C_EXCH + P]).then_inc(bias_loaded, 16)
        act.dma_start(SBIAS[:], bass.AP(scratch.tensor, 0, [[0, P], [GREV, HEADS], [1, PAGE]])).then_inc(sbias_loaded, 16)
        act.wait_ge(sbias_loaded, 16)
        for b in range(4):
            row = N_PAGES * (b + 1) - 1
            act.dma_start(SBIAS[row:row + 1], bass.AP(scratch.tensor, 383, [[0, 1], [GREV, HEADS], [1, PAGE]])
                          ).then_inc(sbias_loaded, 16)

        k_out, v_out = o["k_prompt"], o["v_prompt"]
        for i in range(12):
            tb, what = divmod(i, 3)
            act.wait_ge(tr_done, i + 1)
            if what == 0:
                if tb >= 2:
                    act.wait_ge(k_sent[tb % 2], 16)
                dst = KSTAGE[:, tb % 2]
            else:
                dst = (VT, GVT)[what - 1][:, tb]
            A(dst, PS[:, i % 4], ACT.Copy).then_inc(tr_copied, 1)
            if what < 2:
                act.wait_ge(tr_copied, i + 1)
                t = act.dma_start((k_out, v_out)[what][P * tb:P * tb + P, :], dst)
                t.then_inc(k_sent[tb % 2] if what == 0 else outputs_written, 16)
        for i in range(3):
            act.wait_ge(tr_done, 13 + i)
            if i == 2:
                act.wait_ge(sample_in, 1)
            dst = (KVTOK[:, 0:512], KVTOK[:, 512:1024], GVTOK[:])[i]
            A(dst, PS[0:8, i, :], ACT.Copy).then_inc(tr_copied, 1)
            if i < 2:
                act.wait_ge(tr_copied, 13 + i)
                out_dma((o["k_sample"], o["v_sample"])[i], dst)
        for sent in k_sent:
            act.wait_ge(sent, 32)
        act.wait_ge(outputs_written, 16 * 6)
        act.wait_ge(tr_copied, 15)

        act.wait_ge(sample_in, 1)
        for par in range(2):
            act.dma_start(S0[64 * par:64 * par + 64],
                          a["state_gla"][0].rearrange("b (hp q) k v -> q k b hp v", q=2)[par]).then_inc(s0_loaded, 16)
        act.wait_ge(flip_done, HEADS)
        A(BIAS[:], PS[:, 4:8, :], ACT.Copy).then_inc(bias_ready, 1)
        for hp in range(2):
            act.wait_ge(la_done, hp + 1)
            if hp:
                act.wait_ge(kd_ready, 1)
            link(A(pair(XL[:, 0]), PS[:, 4 + 2 * hp:6 + 2 * hp, 0:HALF], ACT.Identity, bias=VEC2[:, hp:hp + 1]))
            link(A(XL[:, 1], XL[:, 0], ACT.Abs))
            link(A(XL[:, 1], XL[:, 1], ACT.Exp, scale=-1.0))
            A(XL[:, 1], XL[:, 1], ACT.Ln, bias=1.0).then_inc(ln_ready, 1)
            act.wait_ge(bc_ready, hp + 1)
            A(XL[:, 0, 0:SEQ], BC[:, hp], ACT.Exp)
            A(XL[:, 1, 0:SEQ], BC[:, hp], ACT.Exp, scale=-1.0)
            A(DECC[:, hp], BC[:, hp, GLA_CHUNK - 1::GLA_CHUNK], ACT.Exp)
            A(EAS[:, hp], LAS[:, hp], ACT.Exp)
            A(ENS[:, hp], LAS[:, hp], ACT.Exp, scale=-1.0).then_inc(eb_ready, 1)
            act.wait_ge(kdx_ready, hp + 1)
            A(XL[:, 2, 0:SEQ], XL[:, 2, 0:SEQ], ACT.Exp).then_inc(kdx_exp, 1)

        def softmax(g):
            act.wait_ge(snm_ready, g + 1)
            for j in range(8):
                A(SC[g][:, j], SC[g][:, j], ACT.Exp, bias=NROW[:, j:j + 1], accum_out=ROWSUM[:, j:j + 1]).then_inc(soft_done, 1)

        softmax(0)
        for u, (h, qb) in enumerate(UNITS):
            n = P * (qb + 1)
            act.wait_ge(nm_ready, u + 1)
            for c in range(2):
                t = A(PR[:, c, 0:n], PR[:, c, 0:n], ACT.Exp, bias=NM[:, c:c + 1], accum_out=SM[:, c:c + 1])
            t.then_inc(ex_done, 1)
            act.wait_ge(at_done, u + 1)
            A(AT[:, 0:n], PS[:, 2, 0:n], ACT.Copy).then_inc(at_copied, 1)
            act.wait_ge(o_done, u + 1)
            A(PJ[:, h, P * qb:P * qb + P], PS[:, 3, 0:P], ACT.Copy).then_inc(o_copied, 1)

        def past_output(g):
            act.wait_ge(v_used, 32 * (g + 1))
            A(SC[g][0:32, 0:4], PS[0:32, 7, :].rearrange("r (h d) -> r h d", h=HEADS), ACT.Copy).then_inc(og_copied, 1)

        for u, (tb, hp) in enumerate(GLA_UNITS):
            act.wait_ge(kdt_done, u + 1)
            if u:
                act.wait_ge(u_done, u)
            for n in range(8):
                ins = A(KDM[:, n], PS[:, 6, 384:512], ACT.Copy, scale=CHUNKMASK[:, n:n + 1])
            ins.then_inc(kdm_ready, 1)
            if u == 7:
                past_output(0)
            for par in range(2):
                act.wait_ge(go_done, 2 * u + par + 1)
                A(PJ[:, 4 + 2 * hp + par, P * tb:P * tb + P], PS[:, 2 + par, 0:P], ACT.Copy).then_inc(go_copied, 1)
        softmax(1)
        act.wait_ge(st_ready, 64)
        act.wait_ge(gs_v_used, N_SAMPLE)
        for hp in range(2):
            out_dma(o["gla_prompt"][hp], ST[:, hp, 8])
        for par in range(2):
            out_dma(o["gla_sample"].rearrange("b (hp q) k v -> q k b hp v", q=2)[par], S0[64 * par:64 * par + 64])

        for t in range(4):
            A(PJ[:, 20 + t], PJ[:, 20 + t], ACT.Silu).then_inc(silu_ready, 1)
        act.wait_ge(outputs_written, 16 * 10)
        for t in range(KT + 2):
            if t < KT:
                act.wait_ge(mix_held, t + 1)
                A(HSQ[:, t % 2], HSQ[:, t % 2], ACT.Square, scale=2.0 ** -4).then_inc(mix_sq, 1)
            if 1 <= t <= KT:
                q = t - 1
                act.wait_ge(mix_summed, q + 1)
                if q >= 2:
                    act.wait_ge(hf_ready, 8 + q - 1)
                A(HRS[:, q % 2], PS[:, 4 + q % 2, :], ACT.Sqrt, scale=2.0 ** -9, bias=EPSC[:, 1:2]).then_inc(mix_root, 1)
            if t >= 2:
                q = t - 2
                act.wait_ge(hf_ready, 8 + q + 1)
                A(H_hi[:, q, 0:SEQ], HTMP[:, q % 2], ACT.Copy).then_inc(hhi_ready, 1)
        past_output(1)
        act.wait_ge(v_used, 64)
        for i, n in enumerate(("w_gate_a", "w_gate_x")):
            act.dma_start(WG[i][:], a[n][0].rearrange("n d e -> d n e")).then_inc(gates_loaded, 16)
        act.wait_ge(mm_ready, 1)
        A(E1[:], E1[:], ACT.Exp)
        A(E2[:], E2[:], ACT.Exp).then_inc(mm_exp, 1)
        act.wait_ge(h_ready, 16)
        split_hi(Chunk(C_OUT0))
        act.wait_ge(new_held, 1)
        A(MM[:], MM[:], ACT.Square, scale=2.0 ** -4).then_inc(new_sq, 1)
        act.wait_ge(new_summed, 1)
        A(ZZ[:], PS[:, 4, 0:KT * N_SAMPLE], ACT.Sqrt, scale=2.0 ** -9, bias=EPSC[:, 1:2]).then_inc(new_root, 1)
        act.wait_ge(new_scaled, 2)
        A(H_hi[:, :, SEQ:T], E2[:].rearrange("p (k b) -> p k b", k=KT), ACT.Copy).then_inc(new_hi, 1)

        def copies(c0, dst):
            for j in range(4):
                ch = Chunk(c0 + j)
                split_hi(Chunk(c0 + j + 1))
                for i in range(2):
                    if ch.par[i] == 0:
                        act.wait_ge(tiles_done, ch.done[i])
                        A(pair(dst[:, 2 * j + i]), banks(0), ACT.Copy).then_inc(banks_free[0], 1)

        def mlp(layer, c0):
            with act.Fori(0, 4) as g:
                for j in range(8):
                    split_hi(Chunk(c0 + j + 1, g))
                    if j < 4:
                        ch = Chunk(c0 + j, g)
                        for i in range(2):
                            u = 2 * j + i
                            act.wait_ge(banks_free[ch.par[i]], ch.banks_free[i] + 1)
                            if u >= 2:
                                act.wait_ge(u_lo_ready, g * 8 + (32 * layer + u - 1))
                            A(UF[:, i], RL[:, i], ACT.Square).then_inc(uf_ready, 1)

        def acc_ready(c0):
            def ready(eng, kt):
                m = first_tile(c0) + kt
                eng.wait_ge(banks_free[m % 2], m // 2 + 1)
            return ready

        copies(C_OUT0, ACC)
        squares(1, ACC, acc_ready(C_OUT0))
        squares(2, X, x_ready(0), (2, 16, first_tile(C_MLP0)))
        mlp(0, C_MLP0)
        squares(3, ACC, acc_ready(C_IN1 - 4))
        squares(4, X, x_ready(1))
        normed_hi(3, first_tile(C_IN1))

        def gates(kt):
            act.wait_ge(gates_done, kt + 1)
            A(pair(RG[:, kt]), PS[:, 4:6, 0:HALF], ACT.Sigmoid, bias=VEC[:, V_BA + kt:V_BA + kt + 1]).then_inc(r_ready, 1)
            if kt >= 2:
                act.wait_ge(ix_ready, kt - 1)
            A(pair(TMP[:, kt % 2]), PS[:, 6:8, 0:HALF], ACT.Sigmoid, bias=VEC[:, V_BX + kt:V_BX + kt + 1]).then_inc(i_ready, 1)

        act.dma_start(o["conv_sample"][:, 0:2, :], a["state_conv"][0][:, 1:3, :]).then_inc(outputs_written, 16)
        for j in range(8):
            ch = Chunk(C_IN1 + j)
            split_hi(Chunk(C_IN1 + j + 1))
            if j == 0:
                link(A(SPT[:, 0], VEC[:, V_LAM:V_LAM + KT], ACT.Abs))
                link(A(SPT[:, 0], SPT[:, 0], ACT.Exp, scale=-1.0))
                A(SPT[:, 0], SPT[:, 0], ACT.Ln, bias=1.0).then_inc(sp_ln, 1)
            for i in range(2):
                if j < 4 or ch.par[i] == 0:
                    act.wait_ge(tiles_done, ch.done[i])
                    A(pair(GX[:, 2 * j + i]), banks(ch.par[i]), ACT.Gelu_apprx_tanh if j < 4 else ACT.Copy
                      ).then_inc(banks_free[ch.par[i]], 1)
                if j >= 5:
                    gates(2 * (j - 5) + i)
        gates(6)
        gates(7)
        act.wait_ge(spc_ready, 1)
        act.wait_ge(r_ready, KT)
        for kt in range(KT):
            A(DEC[:, kt], RG[:, kt], ACT.Exp, scale=SPC[:, kt:kt + 1])
            A(RG[:, kt], RG[:, kt], ACT.Tanh, scale=SPC[:, kt:kt + 1]).then_inc(th_ready, 1)
        for kt in range(KT):
            act.wait_ge(em_ready, kt + 1)
            A(RG[:, kt], RG[:, kt], ACT.Sqrt, scale=-1.0).then_inc(sqrt_ready, 1)
        act.wait_ge(xrows_done, 1)
        link(A(STOK[:].rearrange("t (b n) -> t b n", b=2), PS[0:11, 6:8, :], ACT.Copy))
        out_dma(o["conv_prompt"], STOK[0:3])
        out_dma(o["conv_sample"][:, 2, :], STOK[3:11])
        act.wait_ge(tiles_done, first_tile(C_OUT1))
        for kt in range(KT):
            act.wait_ge(hf_ready, SCALED_BEFORE[4] + kt + 1)
            A(H_hi[:, kt], TMP[:, kt % 2], ACT.Copy).then_inc(hhi_ready, 1)
        copies(C_OUT1, ACC)
        act.wait_ge(hrows_done, 1)
        act.wait_ge(outputs_written, 16 * 13)
        A(HTOK[0:9].rearrange("t (b n) -> t b n", b=2), PS[0:9, 4:6, :], ACT.Copy).then_inc(hrows_copied, 1)
        act.wait_ge(hrows_copied, 1)
        out_dma(o["rglru_prompt"], HTOK[0:1])
        out_dma(o["rglru_sample"], HTOK[1:9])
        squares(5, ACC, acc_ready(C_OUT1))
        squares(6, X, x_ready(2), (5, 48, first_tile(C_MLP1)))
        mlp(1, C_MLP1)
        squares(7, ACC, acc_ready(N_CHUNKS - 4))
        for tb in range(4):
            act.wait_ge(yt_done, tb + 1)
            if tb >= 2:
                act.wait_ge(y_sent[tb % 2], 16)
            A(YT[:, tb % 2].rearrange("t (b n) -> t b n", b=2), PS[:, 2 * (tb % 2):2 * (tb % 2) + 2, :], ACT.Copy).then_inc(yt_copied, 1)
            act.wait_ge(yt_copied, tb + 1)
            act.dma_start(o["y_prompt"][P * tb:P * tb + P, :], YT[:, tb % 2]).then_inc(y_sent[tb % 2], 16)
        act.wait_ge(yt_done, 5)
        link(A(YS[:].rearrange("t (b n) -> t b n", b=2), PS[0:8, 4:6, :], ACT.Copy))
        out_dma(o["y_sample"], YS[:])
        act.wait_ge(y_sent[0], 32)
        act.wait_ge(y_sent[1], 32)

    @block.vector
    def _(ve):
        chain = [0]

        def link(ins):
            chain[0] += 1
            ins.then_inc(dve_step, 1)
            ve.wait_ge(dve_step, chain[0])

        V = nc.vector
        V.memset(ONES[:], 1.0)
        V.memset(EPSC[:, 0:1], EPS)
        V.memset(EPSC[:, 1:2], EPS / 1024)
        V.memset(TAB[32:33], NEG).then_inc(ones_set, 1)
        ve.wait_ge(idx_loaded, 16)
        for g in range(2):
            V.tensor_scalar(CIDX[g][:], PIDX[:, g:g + 1], 32, None, ALU.mult).then_inc(cidx_ready, 1)

        for i in range(4):
            ve.wait_ge(xt_done, 2 * i + 1)
            V.tensor_copy(X[:, 2 * i, 0:SEQ], PS[:, (2 * i) % 4]).then_inc(xt_copied_even, 1)
        ve.wait_ge(xt_done, 9)
        V.tensor_copy(X[:, :, SEQ:T], PS[:, 4, 0:8 * KT].rearrange("p (k b) -> p k b", k=KT))
        V.tensor_copy(VEC[:], PS[:, 5, 0:P])
        V.tensor_copy(VEC2[:], PS[:, 5, P:P + 4])
        V.tensor_copy(STATE[:], PS[:, 6, 0:256].rearrange("p (k r) -> p k r", k=KT)).then_inc(vec_ready, 1)
        ve.wait_ge(lam_loaded, 64)
        lam_in = LAMIN[:].rearrange("p (a two) d -> p a two d", two=2)
        link(V.tensor_tensor(LAMPR[:], lam_in[:, :, 0], lam_in[:, :, 1], ALU.mult))
        V.tensor_reduce(LAM[:, 0:2], LAMPR[:], AX.X, ALU.add).then_inc(lam_sums, 1)

        def split_lo(ch):
            ve.wait_ge(w_hi_ready, ch.ready)
            V.tensor_tensor(W_lo[:, ch.slot], RAW[:, ch.slot], W_hi[:, ch.slot].bitcast(F32), ALU.subtract).then_inc(w_lo_ready, 1)

        def set_lo(m, kt):
            ve.wait_ge(hhi_ready, 8 * m + kt + 1)
            V.tensor_tensor(H_lo[:, kt], TMP[:, kt % 2], H_hi[:, kt].bitcast(F32), ALU.subtract).then_inc(h_ready, 1)

        def root(n):
            ve.wait_ge(root_ready, n + 1)
            V.reciprocal(RS[:, 1], RS[:, 0]).then_inc(inverse_ready, 1)
            ve.wait_ge(inverse_ready, n + 1)

        def normed(n, m, gain):
            root(n)
            for kt in range(KT + 1):
                if kt < KT:
                    if kt >= 2:
                        ve.wait_ge(h_ready, 8 * m + kt - 1)
                    t = V.scalar_tensor_tensor(TMP[:, kt % 2], X[:, kt], VEC[:, gain + kt:gain + kt + 1], RS[:, 1], ALU.mult, ALU.mult)
                    t.then_inc(hf_ready, 1)
                if kt >= 1:
                    set_lo(m, kt - 1)

        def post(n, i, gain, into=None):
            def lo(kt):
                m, next_gain = into
                ve.wait_ge(hhi_ready, 8 * m + kt + 1)
                V.scalar_tensor_tensor(H_lo[:, kt], X[:, kt], VEC[:, next_gain + kt:next_gain + kt + 1], H_hi[:, kt].bitcast(F32),
                                       ALU.mult, ALU.subtract).then_inc(h_ready, 1)
            root(n)
            for kt in range(0, KT, 2):
                for q in range(2):
                    if kt >= 2:
                        ve.wait_ge(x_odd if q else x_even, 4 * i + kt // 2)
                    t = V.scalar_tensor_tensor(TMP[:, q], ACC[:, kt + q], VEC[:, gain + kt + q:gain + kt + q + 1], RS[:, 1], ALU.mult, ALU.mult)
                    t.then_inc(post_odd if q else post_even, 1)
                ve.wait_ge(post_even, 4 * i + kt // 2 + 1)
                V.tensor_tensor(X[:, kt], X[:, kt], TMP[:, 0], ALU.add).then_inc(x_even, 1)
                if into and kt:
                    lo(kt - 2)
                    lo(kt - 1)
            if into:
                lo(KT - 2)
                lo(KT - 1)

        k_done = [0]

        def k_second(n):
            ve.wait_ge(prod1_ready, n + 1)
            V.tensor_reduce(k_scores(n, 1), PROD[:, 1].rearrange("p n (j d) -> p n j d", d=DH), AX.X, ALU.add).then_inc(prod1_used, 1)

        def k_scores(n, half):
            pos = 4 * (n % 32) + 2 * half
            return SC[n // 32][:, :, pos:pos + 2].rearrange("p j n -> p n j")

        def k_first(n):
            i = place("k", n)
            ve.wait_ge(kv_loaded[i % 4], 16 * (i // 4 + 1))
            V.tensor_tensor(PROD[:, 0], KV[:, i % 4, 0:2, :], QB[:, None, n // 32, :].to_broadcast([P, 2, 512]), ALU.mult).then_inc(k_used, 1)
            ve.wait_ge(k_used, n + 1)
            link(V.tensor_reduce(k_scores(n, 0), PROD[:, 0].rearrange("p n (j d) -> p n j d", d=DH), AX.X, ALU.add))

        def k_chunks(count):
            for _ in range(count):
                n = k_done[0]
                if n % 32:
                    k_second(n - 1)
                k_first(n)
                if n % 32 == 31:
                    k_second(n)
                k_done[0] += 1

        ve.wait_ge(vec_ready, 1)
        root(0)
        x_first_ready(ve, KT - 1)
        for kt in range(KT + 1):
            if kt < KT:
                if kt >= 2:
                    ve.wait_ge(h_ready, kt - 1)
                V.scalar_tensor_tensor(TMP[:, kt % 2], X[:, kt], VEC[:, kt:kt + 1], RS[:, 1], ALU.mult, ALU.mult).then_inc(hf_ready, 1)
            if kt >= 1:
                set_lo(0, kt - 1)
            if kt == KT:
                split_lo(Chunk(0))
        ve.wait_ge(lam_exp, 1)
        link(V.tensor_scalar(LAM[:, 3:4], LAM[:, 1:2], -LAM_INIT, None, ALU.add))
        V.tensor_tensor(LAM[:, 2:3], LAM[:, 3:4], LAM[:, 0:1], ALU.subtract)
        V.tensor_scalar(GD8[:], VEC2[:, 2:3], 1.0 - LAM_INIT, None, ALU.mult)
        for c in range(IN_CHUNKS):
            if c + 1 < IN_CHUNKS:
                split_lo(Chunk(c + 1))
            if c == 3:
                ve.wait_ge(qb_done, 1)
                V.tensor_copy(QB[:, 0], PS[:, 6, :]).then_inc(qb_copied, 1)
                ve.wait_ge(qb_done, 2)
                V.tensor_copy(QB[:, 1], PS[:, 7, :]).then_inc(qb_copied, 1)
                ve.wait_ge(qb_copied, 2)
            if c >= 3:
                k_chunks(2)

        k_chunks(4)
        ve.wait_ge(banks_free[0], 12)
        ve.wait_ge(banks_free[1], 12)
        V.tensor_tensor(QKP[:], PJ[:, 0:4, SEQ:T], PJ[:, 4:8, SEQ:T], ALU.mult)
        V.tensor_copy(VSC[:], PJ[:, 8:12, SEQ:T])
        V.tensor_copy(GVC[:], PJ[:, 16:20, SEQ:T]).then_inc(sample_in, 1)
        ve.wait_ge(sample_in, 1)
        ve.wait_ge(tr_done, 15)
        V.tensor_copy(RSEL[:], IDENT[0:8, 0:8, None].to_broadcast([8, 8, P])).then_inc(rsel_ready, 1)
        link(V.memset(SCANM[:], 1.0))
        link(V.memset(SCANM[:, 0::GLA_CHUNK], 0.0))

        for hp in range(2):
            k_chunks(2)
            ve.wait_ge(ln_ready, hp + 1)
            link(V.tensor_scalar(XL[:, 2], XL[:, 0], 0.0, None, ALU.min))
            link(V.tensor_tensor(XL[:, 2], XL[:, 2], XL[:, 1], ALU.subtract))
            link(V.tensor_scalar(XL[:, 2], XL[:, 2], 1.0 / GLA_TAU, None, ALU.mult))
            V.tensor_copy(LAS[:, hp], XL[:, 2, SEQ:T])
            V.tensor_tensor_scan(BC[:, hp], SCANM[:], XL[:, 2, 0:SEQ], 0.0, ALU.mult, ALU.add).then_inc(bc_ready, 1)
            ve.wait_ge(bc_ready, hp + 1)
            by_chunk = BC[:, hp].rearrange("p (n c) -> p n c", c=GLA_CHUNK)
            V.tensor_tensor(XL[:, 2, 0:SEQ].rearrange("p (n c) -> p n c", c=GLA_CHUNK),
                            by_chunk[:, :, GLA_CHUNK - 1:GLA_CHUNK].to_broadcast([P, SEQ // GLA_CHUNK, GLA_CHUNK]),
                            by_chunk, ALU.subtract).then_inc(kdx_ready, 1)
            k_chunks(2)
            ve.wait_ge(eb_ready, hp + 1)
            V.tensor_tensor(QE[:, hp], PJ[:, 12 + hp, 0:SEQ], XL[:, 0, 0:SEQ], ALU.mult)
            V.tensor_tensor(KE[:, hp], PJ[:, 14 + hp, 0:SEQ], XL[:, 1, 0:SEQ], ALU.mult)
            V.tensor_tensor(QES[:, hp], PJ[:, 12 + hp, SEQ:T], EAS[:, hp], ALU.mult)
            V.tensor_tensor(KES[:, hp], PJ[:, 14 + hp, SEQ:T], ENS[:, hp], ALU.mult)
            link(V.tensor_copy(KSS[:, hp], PJ[:, 14 + hp, SEQ:T]))
            V.tensor_tensor(AKS[:, hp], QES[:, hp], KES[:, hp], ALU.mult)
            ve.wait_ge(kdx_exp, hp + 1)
            V.tensor_tensor(KD[:, hp], PJ[:, 14 + hp, 0:SEQ], XL[:, 2, 0:SEQ], ALU.mult).then_inc(kd_ready, 1)
        V.memset(ST[:, :, 0], 0.0).then_inc(st_first, 1)
        V.memset(ATTM[:], 0.0).then_inc(st_first, 1)
        ve.wait_ge(st_first, 2)

        ve.wait_ge(tb0_loaded, 16)
        ve.wait_ge(nt_done, 1)
        for c in range(2):
            V.tensor_tensor(SN[:].rearrange("p b h c -> p c h b")[:, c], PS[:, 4 + c, 0:32].rearrange("p (h b) -> p h b", h=4),
                            TB0[:, :, None].to_broadcast([P, 4, 8]), ALU.add).then_inc(sn_ready, 1)
        ve.wait_ge(gs_done, 1)
        gv, os_ = GVC[:].rearrange("p (hp q) b -> p q hp b", q=2), OS[:].rearrange("p (hp q) b -> p q hp b", q=2)
        go = PJ[:, 4:8, SEQ:T].rearrange("p (hp q) b -> p q hp b", q=2)
        for par in range(2):
            t = V.tensor_tensor(os_[:, par], gv[:, par], PS[:, par, 0:16].rearrange("p (h b) -> p h b", h=2), ALU.mult)
        link(t)
        for par in range(2):
            V.tensor_tensor(go[:, par], os_[:, par], PS[:, 2 + par, 0:16].rearrange("p (h b) -> p h b", h=2), ALU.add).then_inc(go_s_ready, 1)
        ve.wait_ge(s0_loaded, 32)
        link(V.tensor_tensor(S0[:], S0[:], EAS[:].rearrange("p h b -> p b h")[:, :, :, None].to_broadcast([P, 8, 2, P]), ALU.mult))
        for b in range(N_SAMPLE):
            ve.wait_ge(gs_v_done, b + 1)
            for h in range(HEADS):
                hp, rows = h // 2, slice(64 * (h % 2), 64 * (h % 2) + 64)
                t = V.scalar_tensor_tensor(S0[rows, b, hp], PS[rows, 4 + b % 2, P * h:P * h + P], KSS[rows, hp, b:b + 1],
                                           S0[rows, b, hp], ALU.mult, ALU.add)
            t.then_inc(gs_v_used, 1)

        def softmax(g):
            ve.wait_ge(sbias_loaded, 80)
            ve.wait_ge(prod1_used, k_done[0])
            by_head = SC[g][:].rearrange("p (h c) n -> p h c n", c=2)
            if g:
                ve.wait_ge(smzp_done, 1)
            for c in range(2):
                t = V.tensor_tensor(by_head[:, :, c], by_head[:, :, c], SBIAS[:], ALU.add)
            link(t)
            V.tensor_reduce(ROWMX[:], SC[g][:], AX.X, ALU.max).then_inc(smx_ready, 1)
            ve.wait_ge(smt_done, g + 1)
            link(V.tensor_reduce(M84[:], PS[0:8, 6, 0:P].rearrange("p (b n) -> p b n", b=4), AX.X, ALU.max))
            V.tensor_copy(MEXP[:], M84[:, :, None].to_broadcast([8, 4, 32]))
            V.tensor_tensor(MDIAG[:], M84[:, :, None].to_broadcast([8, 4, 8]),
                            IDENT[0:8, None, 0:8].to_broadcast([8, 4, 8]), ALU.mult).then_inc(smexp_ready, 1)
            ve.wait_ge(smb_done, g + 1)
            V.tensor_scalar(NROW[:], PS[:, 6, 128:136], -1.0, None, ALU.mult).then_inc(snm_ready, 1)
            V.tensor_copy(MP[:, g], PS[:, 6, 256:288].rearrange("p (b j) -> p b j", b=4))
            ve.wait_ge(soft_done, 8 * (g + 1))
            V.tensor_tensor(ZS[:], ROWSUM[:, None, :].to_broadcast([P, 4, 8]), GROUPMASK[:, :, None].to_broadcast([P, 4, 8]),
                            ALU.mult).then_inc(ssum_ready, 1)
            ve.wait_ge(smz_done, g + 1)
            V.tensor_copy(ZP[:, g], PS[:, 6, 288:320].rearrange("p (b j) -> p b j", b=4)).then_inc(smzp_done, 1)

        softmax(0)
        ve.wait_ge(bias_ready, 1)
        for sent in k_sent:
            ve.wait_ge(sent, 32)
        for u, (h, qb) in enumerate(UNITS):
            n = P * (qb + 1)
            ve.wait_ge(sc_done, u + 1)
            if u:
                ve.wait_ge(ad_ready, u)
            for c in range(2):
                t = V.tensor_tensor(PR[:, c, 0:n], PS[:, c, 0:n], BIAS[:, h, 512 - n:512], ALU.add)
            t.then_inc(sc_used, 1)
            ve.wait_ge(sc_used, u + 1)
            link(V.tensor_reduce(MX[:], PR[:, :, 0:n], AX.X, ALU.max))
            V.tensor_scalar(NM[:], MX[:], -1.0, None, ALU.mult).then_inc(nm_ready, 1)
            if u:
                k_second(31 + u)
            ve.wait_ge(ex_done, u + 1)
            link(V.reciprocal(RR[:], SM[:]))
            link(V.tensor_tensor(RR[:, 1:2], RR[:, 1:2], LAM[:, 2:3], ALU.mult))
            if u:
                ve.wait_ge(at_done, u)
            link(V.tensor_scalar(AD[:, 0:n], PR[:, 0, 0:n], RR[:, 0:1], None, ALU.mult))
            V.scalar_tensor_tensor(AD[:, 0:n], PR[:, 1, 0:n], RR[:, 1:2], AD[:, 0:n], ALU.mult, ALU.add).then_inc(ad_ready, 1)
            k_first(32 + u)
        k_done[0] += 16

        def past_output(g):
            ve.wait_ge(ogt_done, g + 1)
            for h in range(HEADS):
                t = V.tensor_copy(PVT[:, h, :, 4 * g:4 * g + 4].rearrange("p c b -> p b c"),
                                  PS[:, 7, 32 * h:32 * h + 32].rearrange("p (b h c) -> p h b c", b=4, h=HEADS)[:, h])
            t.then_inc(pvt_ready, 1)

        for u, (tb, hp) in enumerate(GLA_UNITS):
            k_chunks(1)
            for par in range(2):
                ve.wait_ge(att_done, 2 * u + par + 1)
                if u:
                    ve.wait_ge(go_done, 2 * (u - 1) + par + 1)
                V.copy_predicated(ATTM[:, par], ATTMASK, PS[:, par, 0:P]).then_inc(attm_ready, 1)
            k_chunks(1)
            if tb:
                V.tensor_copy(ST[:, hp, 0], ST[:, hp, 8]).then_inc(st_first, 1)
                ve.wait_ge(st_first, u + 1)
            ve.wait_ge(u_done, u + 1)
            for n in range(8):
                V.scalar_tensor_tensor(ST[:, hp, n + 1], ST[:, hp, n], DECC[:, hp, 8 * tb + n:8 * tb + n + 1],
                                       PS[:, 4 + n // 4, P * (n % 4):P * (n % 4) + P], ALU.mult, ALU.add).then_inc(st_ready, 1)
                ve.wait_ge(st_ready, 8 * u + n + 1)
        past_output(0)
        softmax(1)

        ve.wait_ge(go_copied, 16)
        ve.wait_ge(o_copied, 16)
        for t in range(KT + 2):
            if t < KT:
                if t >= 2:
                    ve.wait_ge(mix_summed, t - 1)
                V.tensor_scalar(HSQ[:, t % 2], PJ[:, t, 0:SEQ], -SQUARE_OVERFLOWS, SQUARE_OVERFLOWS, ALU.max, ALU.min).then_inc(mix_held, 1)
            if 1 <= t <= KT:
                q = t - 1
                ve.wait_ge(mix_root, q + 1)
                link(V.reciprocal(HRS[:, q % 2], HRS[:, q % 2]))
                link(V.tensor_scalar(HUF[:, 0], PS[:, 4 + q % 2, :], SQUARE_OVERFLOWS ** 2 / 256, 1.0 / 32, ALU.is_lt, ALU.mult))
                link(V.tensor_tensor(HRS[:, q % 2], HRS[:, q % 2], HUF[:, 0], ALU.mult))
                gain = GD8[:] if q < 4 else VEC2[:, 3:4]
                if q >= 2:
                    ve.wait_ge(hf_ready, 8 + q)
                    ve.wait_ge(h_ready, 8 + q - 1)
                if q < 4:
                    V.scalar_tensor_tensor(HTMP[:, q % 2], PJ[:, q, 0:SEQ], gain, HRS[:, q % 2], ALU.mult, ALU.mult).then_inc(hf_ready, 1)
                else:
                    link(V.scalar_tensor_tensor(HUF[:, 1], PJ[:, q, 0:SEQ], gain, HRS[:, q % 2], ALU.mult, ALU.mult))
                    ve.wait_ge(silu_ready, q - 3)
                    V.tensor_tensor(HTMP[:, q % 2], HUF[:, 1], PJ[:, 16 + q, 0:SEQ], ALU.mult).then_inc(hf_ready, 1)
            if t >= 2:
                q = t - 2
                ve.wait_ge(hhi_ready, 8 + q + 1)
                V.tensor_tensor(H_lo[:, q, 0:SEQ], HTMP[:, q % 2], H_hi[:, q, 0:SEQ].bitcast(F32), ALU.subtract).then_inc(h_ready, 1)

        mp, zp, sn = (t.rearrange(r) for t, r in ((MP[:], "p g b j -> p (g b j)"), (ZP[:], "p g b j -> p (g b j)"),
                                                  (SN[:], "p b h c -> p (b h c)")))
        ve.wait_ge(smzp_done, 2)
        link(V.tensor_tensor(MM[:], mp, sn, ALU.max))
        V.tensor_tensor(E1[:], mp, MM[:], ALU.subtract)
        V.tensor_tensor(E2[:], sn, MM[:], ALU.subtract).then_inc(mm_ready, 1)
        ve.wait_ge(mm_exp, 1)
        link(V.tensor_tensor(ZZ[:], zp, E1[:], ALU.mult))
        link(V.tensor_tensor(ZZ[:], ZZ[:], E2[:], ALU.add))
        link(V.reciprocal(ZZ[:], ZZ[:]))
        parts = lambda t: t[:].rearrange("p (b h c) -> p c h b", h=4, c=2)
        z1 = ZZ[:].rearrange("p (x c) -> p c x", c=2)[:, 1]
        link(V.tensor_scalar(z1, z1, LAM[:, 2:3], None, ALU.mult))
        V.tensor_tensor(E1[:], E1[:], ZZ[:], ALU.mult)
        link(V.tensor_tensor(E2[:], E2[:], ZZ[:], ALU.mult))
        past_output(1)
        ve.wait_ge(pvt_ready, 2)
        for c in range(2):
            t = V.tensor_tensor(OW[:, c], PVT[:].rearrange("p h c b -> p c h b")[:, c], parts(E1)[:, c], ALU.mult)
        link(V.tensor_tensor(OS[:], parts(E2)[:, 0], parts(E2)[:, 1], ALU.add))
        link(V.tensor_tensor(OW[:, 0], OW[:, 0], OW[:, 1], ALU.add))
        link(V.tensor_tensor(OS[:], OS[:], VSC[:], ALU.mult))
        V.tensor_tensor(PJ[:, 0:4, SEQ:T], OW[:, 0], OS[:], ALU.add).then_inc(sample_o, 1)

        ve.wait_ge(sample_o, 1)
        ve.wait_ge(go_s_ready, 2)
        by_tile = lambda t: t[:].rearrange("p (k b) -> p k b", k=KT)
        V.tensor_scalar(by_tile(MM), PJ[:, 0:KT, SEQ:T], -SQUARE_OVERFLOWS, SQUARE_OVERFLOWS, ALU.max, ALU.min).then_inc(new_held, 1)
        split_lo(Chunk(C_OUT0))
        ve.wait_ge(new_root, 1)
        link(V.reciprocal(ZZ[:], ZZ[:]))
        link(V.tensor_scalar(E1[:], PS[:, 4, 0:KT * N_SAMPLE], SQUARE_OVERFLOWS ** 2 / 256, 1.0 / 32, ALU.is_lt, ALU.mult))
        link(V.tensor_tensor(ZZ[:], ZZ[:], E1[:], ALU.mult))
        V.scalar_tensor_tensor(by_tile(E2)[:, 0:4], PJ[:, 0:4, SEQ:T], GD8[:], by_tile(ZZ)[:, 0:4], ALU.mult, ALU.mult).then_inc(new_scaled, 1)
        link(V.scalar_tensor_tensor(by_tile(E1)[:, 4:8], PJ[:, 4:8, SEQ:T], VEC2[:, 3:4], by_tile(ZZ)[:, 4:8], ALU.mult, ALU.mult))
        V.tensor_tensor(by_tile(E2)[:, 4:8], by_tile(E1)[:, 4:8], PJ[:, 20:24, SEQ:T], ALU.mult).then_inc(new_scaled, 1)
        ve.wait_ge(new_hi, 1)
        V.tensor_tensor(H_lo[:, :, SEQ:T], by_tile(E2), H_hi[:, :, SEQ:T].bitcast(F32), ALU.subtract).then_inc(new_ready, 1)

        def copies(c0, dst):
            for j in range(4):
                ch = Chunk(c0 + j)
                split_lo(Chunk(c0 + j + 1))
                for i in range(2):
                    if ch.par[i] == 1:
                        ve.wait_ge(tiles_done, ch.done[i])
                        V.tensor_copy(pair(dst[:, 2 * j + i]), banks(1)).then_inc(banks_free[1], 1)

        def mlp(layer, c0):
            link(V.memset(ACC[:], 0.0))
            with ve.Fori(0, 4) as g:
                for j in range(8):
                    split_lo(Chunk(c0 + j + 1, g))
                    ch = Chunk(c0 + j, g)
                    if j < 4:
                        for i in range(2):
                            u = 32 * layer + 2 * j + i
                            ve.wait_ge(tiles_done, ch.done[i])
                            V.scalar_tensor_tensor(pair(RL[:, i]), banks(ch.par[i]), 0.0, pair(RS[:, 1]), ALU.max, ALU.mult
                                                   ).then_inc(banks_free[ch.par[i]], 1)
                            ve.wait_ge(uf_ready, g * 8 + (u + 1))
                            V.tensor_copy(U_hi[:, 2 * j + i], UF[:, i]).then_inc(u_hi_ready, 1)
                            ve.wait_ge(u_hi_ready, g * 8 + (u + 1))
                            V.tensor_tensor(U_lo[:, 2 * j + i], UF[:, i], U_hi[:, 2 * j + i].bitcast(F32), ALU.subtract).then_inc(u_lo_ready, 1)
                    else:
                        for i in range(2):
                            m = 2 * (j - 4) + i
                            ve.wait_ge(tiles_done, ch.done[i])
                            V.tensor_tensor(pair(ACC[:, m]), pair(ACC[:, m]), banks(ch.par[i]), ALU.add).then_inc(banks_free[ch.par[i]], 1)

        copies(C_OUT0, ACC)
        post(1, 0, 8, (2, 16))
        root(2)
        mlp(0, C_MLP0)
        post(3, 1, 24)
        normed(4, 3, 32)

        def convolution(kt):
            xb = GX[:, KT + kt]
            w = lambda j: VEC[:, V_CONVW + 8 * j + kt:V_CONVW + 8 * j + kt + 1]
            mt = first_tile(C_IN1) + KT + kt
            ve.wait_ge(banks_free[mt % 2], mt // 2 + 1)
            if kt >= 2:
                ve.wait_ge(gates_done, kt - 1)
                ve.wait_ge(ix_ready, kt - 1)
            xc = XC[:, kt % 2]
            link(V.tensor_scalar(xc, xb, w(3), VEC[:, V_CONVB + kt:V_CONVB + kt + 1], ALU.mult, ALU.add))
            for j in (2, 1, 0):
                back = CONV_W - 1 - j
                V.scalar_tensor_tensor(xc[:, back:SEQ], xb[:, 0:SEQ - back], w(j), xc[:, back:SEQ], ALU.mult, ALU.add)
                t = V.scalar_tensor_tensor(xc[:, SEQ:T], STATE[:, kt, j:24:3], w(j), xc[:, SEQ:T], ALU.mult, ALU.add)
                if j:
                    link(t)
            t.then_inc(xc_ready, 1)
            if kt:
                input_gate(ve, kt - 1)

        for j in range(8):
            ch = Chunk(C_IN1 + j)
            split_lo(Chunk(C_IN1 + j + 1))
            if j == 1:
                ve.wait_ge(sp_ln, 1)
                link(V.tensor_scalar(SPT[:, 1], VEC[:, V_LAM:V_LAM + KT], -1.0, 0.0, ALU.mult, ALU.max))
                link(V.tensor_tensor(SPT[:, 1], SPT[:, 1], SPT[:, 0], ALU.add))
                V.tensor_scalar(SPC[:], SPT[:, 1], -RG_C, None, ALU.mult).then_inc(spc_ready, 1)
            for i in range(2):
                if j >= 5:
                    convolution(2 * (j - 5) + i)
                if j >= 4 and ch.par[i] == 1:
                    ve.wait_ge(tiles_done, ch.done[i])
                    V.tensor_copy(pair(GX[:, 2 * j + i]), banks(1)).then_inc(banks_free[1], 1)
        convolution(6)
        convolution(7)
        input_gate(ve, KT - 1)
        for kt in range(KT):
            ve.wait_ge(th_ready, kt + 1)
            if kt >= 2:
                ve.wait_ge(em_ready, kt - 1)
            link(V.tensor_tensor(SQ[:, kt % 2], DEC[:, kt], DEC[:, kt], ALU.mult))
            V.scalar_tensor_tensor(RG[:, kt], SQ[:, kt % 2], 1.0, RG[:, kt], ALU.add, ALU.mult).then_inc(em_ready, 1)
        for kt in range(KT):
            ve.wait_ge(sqrt_ready, kt + 1)
            link(V.tensor_tensor(INP[:, kt], INP[:, kt], RG[:, kt], ALU.mult))
            V.tensor_tensor_scan(RG[:, kt, 0:SEQ], DEC[:, kt, 0:SEQ], INP[:, kt, 0:SEQ], 0.0, ALU.mult, ALU.add)
            link(V.tensor_tensor(RG[:, kt, SEQ:T], DEC[:, kt, SEQ:T], STATE[:, kt, 24:32], ALU.mult))
            link(V.tensor_tensor(RG[:, kt, SEQ:T], RG[:, kt, SEQ:T], INP[:, kt, SEQ:T], ALU.add))
            V.tensor_copy(HL[:, kt], RG[:, kt, SEQ - 1:T]).then_inc(hl_ready, 1)
            mt = first_tile(C_IN1) + kt
            ve.wait_ge(banks_free[mt % 2], mt // 2 + 1)
            ve.wait_ge(hl_ready, kt + 1)
            if kt >= 2:
                ve.wait_ge(h_ready, 32 + kt - 1)
            V.tensor_tensor(TMP[:, kt % 2], GX[:, kt], RG[:, kt], ALU.mult).then_inc(hf_ready, 1)
            if kt >= 1:
                set_lo(4, kt - 1)
        set_lo(4, KT - 1)

        copies(C_OUT1, ACC)
        post(5, 2, 40, (5, 48))
        root(6)
        mlp(1, C_MLP1)
        post(7, 3, 56)

    @block.tensor
    def _(pe):
        MM_ = nc.tensor.matmul
        TR = nc.tensor.transpose

        pe.wait_ge(const_loaded, 16)
        pe.wait_ge(x_loaded, 16 * 5)
        for kt in range(KT):
            if kt >= 4:
                pe.wait_ge((xt_copied_even, xt_copied_odd)[kt % 2], (kt - 4) // 2 + 1)
            for tb in range(4):
                t = TR(PS[:, kt % 4, P * tb:P * tb + P], XIN[:, tb, P * kt:P * kt + P], IDENT)
            t.then_inc(xt_done, 1)
        pe.wait_ge(rows_loaded, 16 * 11)
        for kt in range(KT):
            TR(PS[:, 4, 8 * kt:8 * kt + 8], XSIN[:, P * kt:P * kt + P], IDENT[0:8, 0:8])
            TR(PS[:, 6, 32 * kt:32 * kt + 32], SROWS[:, P * kt:P * kt + P], IDENT[0:32, 0:32])
        TR(PS[:, 5, 0:P], VROWS[:], IDENT)
        TR(PS[:, 5, P:P + 4], VROWS2[:], IDENT[0:4, 0:4]).then_inc(xt_done, 1)
        pe.wait_ge(ones_set, 1)
        pe.wait_ge(tab_loaded, 32)
        pe.wait_ge(vec_ready, 1)
        MM_(PS[0:4, 7, :], TAB[:], HOT[:, 0:512], start=True, stop=True)
        MM_(PS[0:4, 6, 256:384], TAB[:], HOT[:, 512:GREV], start=True, stop=True).then_inc(g_done, 1)

        def sum_squares(n):
            if n >= 1:
                pe.wait_ge(root_ready, n)
            for kt in range(KT):
                pe.wait_ge(sq_ready, 8 * n + kt + 1)
                for i, half in enumerate(halves):
                    t = MM_(PS[:, 4 + i, 0:HALF], ONES[:], SQ[:, kt % 2, half], start=kt == 0, stop=kt == KT - 1)
                t.then_inc(sq_summed, 1)

        def products(ch, hi, lo, ready=None, after=None):
            pe.wait_ge(w_lo_ready, ch.ready)
            for i in range(ch.count):
                if ch.tiles[i] >= 2:
                    pe.wait_ge(banks_free[ch.par[i]], ch.banks_free[i])
                cols = slice(P * i, P * i + P)
                for k in range(KT):
                    if ready and i == 0:
                        ready(k)
                    for n, (w, x) in enumerate(((W_hi, hi), (W_hi, lo), (W_lo, hi))):
                        for j, half in enumerate(halves):
                            t = MM_(PS[:, 2 * ch.par[i] + j, 0:HALF], w[:, ch.slot, k, cols], x[:, k, half],
                                    start=k == 0 and n == 0, stop=k == KT - 1 and n == 2)
                t.then_inc(tiles_done, 1)
                if after:
                    after(i)

        def set_ready(m):
            return lambda k: pe.wait_ge(h_ready, 8 * m + k + 1)

        def stage(c0, count, m):
            for j in range(count):
                products(Chunk(c0 + j), H_hi, H_lo, set_ready(m) if j == 0 else None)

        def mlp(layer, c0, m):
            pe.wait_ge(h_ready, 8 * m + 8)
            with pe.Fori(0, 4) as g:
                for j in range(4):
                    products(Chunk(c0 + j, g), H_hi, H_lo)
                for j in range(4, 8):
                    products(Chunk(c0 + j, g), U_hi, U_lo,
                             (lambda k: pe.wait_ge(u_lo_ready, g * 8 + (32 * layer + k + 1))) if j == 4 else None)

        sum_squares(0)
        for c in range(IN_CHUNKS):
            products(Chunk(c), H_hi, H_lo, set_ready(0) if c == 0 else None)
            if c == 2:
                pe.wait_ge(banks_free[0], 2)
                pe.wait_ge(banks_free[1], 2)
                pe.wait_ge(scratch_written, 16)
                for h in range(HEADS):
                    t = TR(PS[0:8, 6, P * h:P * h + P], PJ[:, h, SEQ:T], IDENT)
                t.then_inc(q_rows_done, 1)
            if c == 3:
                pe.wait_ge(q_rows_copied, 1)
                for g in range(2):
                    MM_(PS[:, 6 + g, :], CONST[0:8, C_SEL + P * g:C_SEL + P * g + P], QTOK[:], start=True, stop=True).then_inc(qb_done, 1)

        pe.wait_ge(banks_free[0], 13)
        pe.wait_ge(banks_free[1], 12)
        for i in range(12):
            tb, what = divmod(i, 3)
            if i >= 4:
                pe.wait_ge(tr_copied, i - 3)
            for h in range(HEADS):
                t = TR(PS[:, i % 4, P * h:P * h + P], PJ[:, (4, 8, 16)[what] + h, P * tb:P * tb + P], IDENT)
            t.then_inc(tr_done, 1)
        pe.wait_ge(tr_copied, 12)
        for i, off in enumerate((4, 8, 16)):
            for h in range(HEADS):
                t = TR(PS[0:8, i, P * h:P * h + P], PJ[:, off + h, SEQ:T], IDENT)
            t.then_inc(tr_done, 1)
        pe.wait_ge(bias_loaded, 32)
        pe.wait_ge(qb_copied, 2)
        for h in range(HEADS):
            MM_(PS[:, 4 + h, :], EXCHANGE[:], FLIPPED[:, h], start=True, stop=True).then_inc(flip_done, 1)
        pe.wait_ge(bias_ready, 1)
        pe.wait_ge(wa2_loaded, 16)
        pe.wait_ge(qb_copied, 2)
        for hp in range(2):
            for i, half in enumerate(halves):
                t = MM_(PS[:, 4 + 2 * hp + i, 0:HALF], WA2[:, P * hp:P * hp + P], LR[0:RANK, half], start=True, stop=True)
            t.then_inc(la_done, 1)
        pe.wait_ge(sample_in, 1)
        pe.wait_ge(ln_ready, 1)
        for c in range(2):
            rows = slice(64 * c, 64 * c + 64)
            t = MM_(PS[:, 4 + c, 0:32], ONES[rows], QKP[rows].rearrange("p h b -> p (h b)"), start=True, stop=True)
        t.then_inc(nt_done, 1)
        pe.wait_ge(kd_ready, 2)
        pe.wait_ge(tr_copied, 15)
        for par in range(2):
            rows = slice(64 * par, 64 * par + 64)
            MM_(PS[:, par, 0:16], ONES[rows], AKS[rows].rearrange("p h b -> p (h b)"), start=True, stop=True)
        pe.wait_ge(s0_loaded, 32)
        for par in range(2):
            rows = slice(64 * par, 64 * par + 64)
            for hp in range(2):
                for b in range(N_SAMPLE):
                    t = MM_(PS[:, 2 + par, 8 * hp + b:8 * hp + b + 1], S0[rows, b, hp], QES[rows, hp, b:b + 1], start=True, stop=True)
        t.then_inc(gs_done, 1)
        pe.wait_ge(rsel_ready, 1)
        pe.wait_ge(sn_ready, 2)
        for b in range(N_SAMPLE):
            if b >= 2:
                pe.wait_ge(gs_v_used, b - 1)
            MM_(PS[:, 4 + b % 2, :], RSEL[:, b], GVTOK[:], start=True, stop=True).then_inc(gs_v_done, 1)

        def scores(u):
            h, qb = UNITS[u]
            if u:
                pe.wait_ge(sc_used, u)
            for c in range(2):
                rows = slice(64 * c, 64 * c + 64)
                t = MM_(PS[:, c, 0:P * (qb + 1)], PJ[rows, h, P * qb:P * qb + P], PJ[rows, 4 + h, 0:P * (qb + 1)], start=True, stop=True)
            t.then_inc(sc_done, 1)

        def softmax(g):
            pe.wait_ge(smx_ready, g + 1)
            TR(PS[0:8, 6, 0:P], ROWMX[:], IDENT).then_inc(smt_done, 1)
            pe.wait_ge(smexp_ready, g + 1)
            TR(PS[:, 6, 128:136], MEXP[:].rearrange("j b n -> j (b n)"), IDENT[0:8, 0:8])
            MM_(PS[:, 6, 256:288], ONES[0:8], MDIAG[:].rearrange("j b i -> j (b i)"), start=True, stop=True).then_inc(smb_done, 1)
            pe.wait_ge(ssum_ready, g + 1)
            MM_(PS[:, 6, 288:320], ONES[:], ZS[:].rearrange("p b j -> p (b j)"), start=True, stop=True).then_inc(smz_done, 1)

        def v_chunks(n0, count):
            for n in range(n0, n0 + count):
                i, g = place("v", n), n // 32
                pe.wait_ge(kv_loaded[i % 4], 16 * (i // 4 + 1))
                pe.wait_ge(pm_ready, n // 4 + 1)
                for pos in range(4):
                    t = MM_(PS[0:32, 7, :], PM[:, (n // 4) % 2, 4 * (n % 4) + pos].rearrange("p b j -> p (b j)"),
                            KV[:, i % 4, pos, :], start=n % 32 == 0 and pos == 0, stop=n % 32 == 31 and pos == 3)
                t.then_inc(v_used, 1)
                if n % 32 == 31:
                    pe.wait_ge(og_copied, g + 1)
                    for h in range(HEADS):
                        t = TR(PS[:, 7, 32 * h:32 * h + 32], SC[g][0:32, h, :], IDENT[0:32, 0:32])
                    t.then_inc(ogt_done, 1)
                if n == 32 - 1:
                    pe.wait_ge(pvt_ready, 1)

        softmax(0)
        pe.wait_ge(go_s_ready, 2)
        scores(0)
        for u, (h, qb) in enumerate(UNITS):
            if u + 1 < len(UNITS):
                scores(u + 1)
            v_chunks(u, 1)
            pe.wait_ge(ad_ready, u + 1)
            if u:
                pe.wait_ge(at_copied, u)
            for kb in range(qb + 1):
                t = TR(PS[:, 2, P * kb:P * kb + P], AD[:, P * kb:P * kb + P], IDENT)
            t.then_inc(at_done, 1)
            pe.wait_ge(at_copied, u + 1)
            if u:
                pe.wait_ge(o_copied, u)
            for kb in range(qb + 1):
                t = MM_(PS[:, 3, 0:P], VT[:, kb, P * h:P * h + P], AT[:, P * kb:P * kb + P], start=kb == 0, stop=kb == qb)
            t.then_inc(o_done, 1)
        pe.wait_ge(o_copied, len(UNITS))

        for u, (tb, hp) in enumerate(GLA_UNITS):
            block_cols = slice(P * tb, P * tb + P)
            if u:
                pe.wait_ge(kdm_ready, u)
            TR(PS[:, 6, 384:512], KD[:, hp, block_cols], IDENT).then_inc(kdt_done, 1)
            for par in range(2):
                rows = slice(64 * par, 64 * par + 64)
                if u:
                    pe.wait_ge(attm_ready, 2 * (u - 1) + par + 1)
                MM_(PS[:, par, 0:P], KE[rows, hp, block_cols], QE[rows, hp, block_cols], start=True, stop=True).then_inc(att_done, 1)
            v_chunks(16 + 2 * u, 1)
            pe.wait_ge(kdm_ready, u + 1)
            if u:
                pe.wait_ge(st_ready, 8 * u)
            for n in range(8):
                for par in range(2):
                    h, rows = 2 * hp + par, slice(64 * par, 64 * par + 64)
                    t = MM_(PS[rows, 4 + n // 4, P * (n % 4):P * (n % 4) + P], KDM[:, n, 64 * par:64 * par + 64],
                            GVT[:, tb, P * h:P * h + P], start=True, stop=True)
            t.then_inc(u_done, 1)
            v_chunks(17 + 2 * u, 1)
            for par in range(2):
                h, rows = 2 * hp + par, slice(64 * par, 64 * par + 64)
                pe.wait_ge(attm_ready, 2 * u + par + 1)
                if u:
                    pe.wait_ge(go_copied, 2 * (u - 1) + par + 1)
                MM_(PS[:, 2 + par, 0:P], GVT[:, tb, P * h:P * h + P], ATTM[:, par], start=True, stop=False)
                for n in range(8):
                    if n:
                        pe.wait_ge(st_ready, 8 * u + n)
                    else:
                        pe.wait_ge(st_first, max(2, u + 1))
                    t = MM_(PS[:, 2 + par, GLA_CHUNK * n:GLA_CHUNK * n + GLA_CHUNK], ST[rows, hp, n],
                            QE[rows, hp, P * tb + GLA_CHUNK * n:P * tb + GLA_CHUNK * (n + 1)], start=False, stop=n == 7)
                t.then_inc(go_done, 1)
        softmax(1)
        pe.wait_ge(st_ready, 64)
        for t_ in range(KT):
            v_chunks(32 + 3 * t_, 3)
            pe.wait_ge(mix_sq, t_ + 1)
            if t_ >= 2:
                pe.wait_ge(hf_ready, 8 + t_ - 1)
            MM_(PS[:, 4 + t_ % 2, :], ONES[:], HSQ[:, t_ % 2], start=True, stop=True).then_inc(mix_summed, 1)
        v_chunks(56, 8)
        pe.wait_ge(hf_ready, 16)
        pe.wait_ge(new_sq, 1)
        MM_(PS[:, 4, 0:KT * N_SAMPLE], ONES[:], MM[:], start=True, stop=True).then_inc(new_summed, 1)
        pe.wait_ge(new_ready, 1)
        stage(C_OUT0, 4, 1)
        sum_squares(1)
        sum_squares(2)
        mlp(0, C_MLP0, 2)
        sum_squares(3)
        sum_squares(4)

        def gates(kt):
            pe.wait_ge(xc_ready, kt + 1)
            if kt:
                pe.wait_ge(r_ready, kt)
                pe.wait_ge(i_ready, kt)
            else:
                pe.wait_ge(gates_loaded, 32)
            for w in range(2):
                for i, half in enumerate(halves):
                    t = MM_(PS[:, 4 + 2 * w + i, 0:HALF], WG[w][:, kt], XC[:, kt % 2, half], start=True, stop=True)
            t.then_inc(gates_done, 1)

        for j in range(8):
            products(Chunk(C_IN1 + j), H_hi, H_lo, set_ready(3) if j == 0 else None,
                     (lambda i: gates(2 * (j - 5) + i)) if j >= 5 else None)
        gates(6)
        gates(7)
        pe.wait_ge(banks_free[0], first_tile(C_OUT1) // 2 + first_tile(C_OUT1) % 2)
        pe.wait_ge(banks_free[1], first_tile(C_OUT1) // 2)
        pe.wait_ge(i_ready, KT)
        for kt in range(KT):
            t = TR(PS[0:11, 6 + kt // 4, P * (kt % 4):P * (kt % 4) + P], GX[:, KT + kt, SEQ - 3:T], IDENT)
        t.then_inc(xrows_done, 1)
        stage(C_OUT1, 4, 4)
        pe.wait_ge(hl_ready, KT)
        for kt in range(KT):
            t = TR(PS[0:9, 4 + kt // 4, P * (kt % 4):P * (kt % 4) + P], HL[:, kt], IDENT)
        t.then_inc(hrows_done, 1)
        pe.wait_ge(hrows_copied, 1)
        sum_squares(5)
        sum_squares(6)
        mlp(1, C_MLP1, 5)
        sum_squares(7)
        pe.wait_ge(x_even, 16)
        pe.wait_ge(x_odd, 16)
        for tb in range(4):
            if tb >= 2:
                pe.wait_ge(yt_copied, tb - 1)
            for kt in range(KT):
                t = TR(PS[:, 2 * (tb % 2) + kt // 4, P * (kt % 4):P * (kt % 4) + P], X[:, kt, P * tb:P * tb + P], IDENT)
            t.then_inc(yt_done, 1)
        pe.wait_ge(root_ready, 8)
        for kt in range(KT):
            t = TR(PS[0:8, 4 + kt // 4, P * (kt % 4):P * (kt % 4) + P], X[:, kt, SEQ:T], IDENT)
        t.then_inc(yt_done, 1)


_OUTS = [("y_prompt", (1, SEQ, D_MODEL)), ("y_sample", (N_SAMPLE, 1, D_MODEL)),
         ("k_prompt", (1, 1, SEQ, HEADS, P)), ("v_prompt", (1, 1, SEQ, HEADS, P)),
         ("k_sample", (1, N_SAMPLE, 1, HEADS, P)), ("v_sample", (1, N_SAMPLE, 1, HEADS, P)),
         ("gla_prompt", (1, 1, HEADS, DH, P)), ("gla_sample", (1, N_SAMPLE, HEADS, DH, P)),
         ("conv_prompt", (1, 1, CONV_W - 1, D_MODEL)), ("conv_sample", (1, N_SAMPLE, CONV_W - 1, D_MODEL)),
         ("rglru_prompt", (1, 1, D_MODEL)), ("rglru_sample", (1, N_SAMPLE, D_MODEL))]


def build(nc, a, o):
    views = {
        "y_prompt": o["y_prompt"][0], "y_sample": o["y_sample"].rearrange("b t d -> (b t) d"),
        "k_prompt": o["k_prompt"][0, 0].rearrange("t h d -> t (h d)"), "v_prompt": o["v_prompt"][0, 0].rearrange("t h d -> t (h d)"),
        "k_sample": o["k_sample"][0].rearrange("b t h d -> (b t) (h d)"), "v_sample": o["v_sample"][0].rearrange("b t h d -> (b t) (h d)"),
        "gla_prompt": o["gla_prompt"][0, 0].rearrange("(hp q) k v -> hp (q k) v", q=2), "gla_sample": o["gla_sample"][0],
        "conv_prompt": o["conv_prompt"][0, 0], "conv_sample": o["conv_sample"][0],
        "rglru_prompt": o["rglru_prompt"][0], "rglru_sample": o["rglru_sample"][0]}
    with ExitStack() as ctx:
        trunk(nc, ctx, a, views)


def kernel(**inputs):
    import numpy as _np
    import concourse.bacc as _bacc
    from concourse import mybir as _mybir
    from concourse.bass_utils import run_bass_kernel_spmd as _run

    nc = _bacc.Bacc("TRN2", target_bir_lowering=False, num_devices=1)
    arrays, args, outs = {}, {}, {}
    for name, x in [*inputs.items(), ("consts", constant_table())]:
        x = _np.ascontiguousarray(x)
        arrays[f"in_{name}"] = x
        args[name] = nc.dram_tensor(f"in_{name}", x.shape, _mybir.dt.from_np(x.dtype), kind="ExternalInput").ap()
    for name, shape in _OUTS:
        outs[name] = nc.dram_tensor(f"out_{name}", shape, _mybir.dt.float32, kind="ExternalOutput").ap()
    build(nc, args, outs)
    r = _run(nc, [arrays], core_ids=[0])
    return tuple(r.results[0][f"out_{name}"] for name, _ in _OUTS)
```
